# Optimizing a Trainium2 kernel written in Bass

```python
import jax
import jax.numpy as jnp
from jax import lax
import numpy as np

D_MODEL = 1024
BATCH = 1
SEQ = 256
DEPTH = 2
DEC_BATCH = 1
DEC_SEQ = 256
PAST_LEN = 128

RG_WIDTH = D_MODEL // 2
RG_BLOCKS = 8
RG_BLOCK_DIM = RG_WIDTH // RG_BLOCKS
CONV_WIDTH = 4
RG_C = 8.0
RW_HEADS = 8
RW_HEAD_DIM = (D_MODEL // 2) // RW_HEADS
RW_WIDTH = RW_HEADS * RW_HEAD_DIM
DECAY_LORA = 32
ICL_LORA = 32
GATE_LORA = 64
RW_IN = 3 * RW_WIDTH + DECAY_LORA + ICL_LORA + GATE_LORA
REC_IN = 2 * RG_WIDTH + RW_IN
RW_GN_EPS = 64e-5
ATT_HEADS = 16
ATT_KV_HEADS = 4
ATT_GROUP = ATT_HEADS // ATT_KV_HEADS
ATT_HEAD_DIM = D_MODEL // ATT_HEADS
WINDOW = 128
ATT_BLOCK = 128
KEY_SPAN = ATT_BLOCK + 2 * WINDOW
ATT_IN = (ATT_HEADS + 2 * ATT_KV_HEADS) * ATT_HEAD_DIM
N_GROUPS = 4
EXPERTS_PER_GROUP = 8
N_EXPERTS = N_GROUPS * EXPERTS_PER_GROUP
TOP_K = 2
EXPERT_FF = 512
MOE_BLOCK = 128

RMS_EPS = 1e-6
NEG_INF = -1e30
N_REC = (DEPTH + 1) // 2
N_ATT = DEPTH // 2

kernel_name = "hybrid_bidir_rglru_rwkv7_swa_hmoe"

def rms_norm(x, g):
    xf = x.astype(jnp.float32)
    y = xf * lax.rsqrt(jnp.mean(xf * xf, -1, keepdims=True) + RMS_EPS)
    return (y * g.astype(jnp.float32)).astype(x.dtype)

def head_rms(x, g):
    xf = x.astype(jnp.float32)
    y = xf * lax.rsqrt(jnp.mean(xf * xf, -1, keepdims=True) + RMS_EPS)
    return (y * g.astype(jnp.float32)).astype(x.dtype)

def depthwise_conv(x, w, b):
    left = CONV_WIDTH // 2
    y = lax.conv_general_dilated(
        x, w[:, None, :].astype(x.dtype), window_strides=(1,),
        padding=[(left, CONV_WIDTH - 1 - left)],
        dimension_numbers=('NWC', 'WIO', 'NWC'), feature_group_count=x.shape[-1])
    return y + b

def _lin_combine(left, right):
    a_l, b_l = left
    a_r, b_r = right
    return a_l * a_r, a_r * b_l + b_r

def rglru(xc, wa, ba, wx, bx, lam):
    B, S, _ = xc.shape
    f32 = jnp.float32
    xf = xc.astype(f32)
    xb = xf.reshape(B, S, RG_BLOCKS, RG_BLOCK_DIM)
    r = jax.nn.sigmoid(jnp.einsum('bsnc,ncd->bsnd', xb, wa.astype(f32)).reshape(B, S, RG_WIDTH) + ba)
    i = jax.nn.sigmoid(jnp.einsum('bsnc,ncd->bsnd', xb, wx.astype(f32)).reshape(B, S, RG_WIDTH) + bx)
    log_a = -RG_C * r * jax.nn.softplus(-lam.astype(f32))
    a = jnp.exp(log_a)
    b = jnp.sqrt(-jnp.expm1(2.0 * log_a)) * (i * xf)
    return lax.associative_scan(_lin_combine, (a, b), axis=1)[1]

def centred_shift_mix(u, mu_l, mu_r):
    prev = jnp.pad(u, ((0, 0), (1, 0), (0, 0)))[:, :-1]
    nxt = jnp.pad(u, ((0, 0), (0, 1), (0, 0)))[:, 1:]
    return u + mu_l * (prev - u) + mu_r * (nxt - u)

def wkv_scan(r, w, k, v, kk, a, reverse):
    B, S, H, N = r.shape
    xs = tuple(jnp.moveaxis(t, 1, 0) for t in (r, w, k, v, kk, a))

    def step(state, inp):
        r_t, w_t, k_t, v_t, kk_t, a_t = inp
        sa = jnp.einsum('bhij,bhj->bhi', state, -kk_t)
        state = (state * w_t[:, :, None, :]
                 + sa[..., :, None] * (kk_t * a_t)[:, :, None, :]
                 + v_t[..., :, None] * k_t[:, :, None, :])
        y = jnp.einsum('bhij,bhj->bhi', state, r_t)
        return state, y

    state0 = jnp.zeros((B, H, N, N), jnp.float32)
    _, ys = lax.scan(step, state0, xs, reverse=reverse)
    return jnp.moveaxis(ys, 0, 1)

def recurrent_mixer(h, w_in, conv_w, conv_b, rg_wa, rg_ba, rg_wx, rg_bx, rg_lambda,
                    mu_l, mu_r, w0, w_up, a0, a_up, g_up, k_k, k_a, r_k, ln_w, ln_b, w_out):
    B, S, _ = h.shape
    f32 = jnp.float32
    u = h @ w_in
    rg_x, rg_g, rw = jnp.split(u, [RG_WIDTH, 2 * RG_WIDTH], axis=-1)

    xc = depthwise_conv(rg_x, conv_w, conv_b)
    h_fwd = rglru(xc, rg_wa[0], rg_ba[0], rg_wx[0], rg_bx[0], rg_lambda[0])
    h_bwd = jnp.flip(rglru(jnp.flip(xc, 1), rg_wa[1], rg_ba[1], rg_wx[1], rg_bx[1], rg_lambda[1]), 1)
    rg_out = (h_fwd + h_bwd) * jax.nn.gelu(rg_g.astype(f32))

    rw = centred_shift_mix(rw, mu_l, mu_r).astype(f32)
    r, k, v, wd, ad, gd = jnp.split(
        rw, [RW_WIDTH, 2 * RW_WIDTH, 3 * RW_WIDTH, 3 * RW_WIDTH + DECAY_LORA,
             3 * RW_WIDTH + DECAY_LORA + ICL_LORA], axis=-1)

    def heads(t):
        return t.reshape(B, S, RW_HEADS, RW_HEAD_DIM)

    kk = heads(k * k_k)
    kk = kk / jnp.maximum(jnp.sqrt(jnp.sum(kk * kk, -1, keepdims=True)), 1e-12)
    tw = jnp.tanh(wd)

    def direction(d, reverse):
        w_log = -jax.nn.softplus(-(w0[d] + tw @ w_up[d].astype(f32))) - 0.5
        decay = jnp.exp(-jnp.exp(w_log))
        a = jax.nn.sigmoid(a0[d] + ad @ a_up[d].astype(f32))
        kd = k * (1.0 + (a - 1.0) * k_a)
        y = wkv_scan(heads(r), heads(decay), heads(kd), heads(v), kk, heads(a), reverse)
        return y, kd

    y_f, k_f = direction(0, False)
    y_b, k_b = direction(1, True)
    y = y_f + y_b
    mu = jnp.mean(y, -1, keepdims=True)
    var = jnp.mean(jnp.square(y - mu), -1, keepdims=True)
    yn = ((y - mu) * lax.rsqrt(var + RW_GN_EPS)).reshape(B, S, RW_WIDTH) * ln_w + ln_b
    bonus = jnp.sum(heads(r) * heads(k_f + k_b) * r_k, -1, keepdims=True) * heads(v)
    g = jax.nn.sigmoid(gd) @ g_up.astype(f32)
    rw_out = (yn + bonus.reshape(B, S, RW_WIDTH)) * g

    mixed = jnp.concatenate([rg_out, rw_out], axis=-1).astype(h.dtype)
    return mixed @ w_out

def alibi_slopes():
    return 2.0 ** (-8.0 * jnp.arange(1, ATT_HEADS + 1, dtype=jnp.float32) / ATT_HEADS)

def window_attention(h, w_in, q_norm, k_norm, sink, w_out):
    B, S, _ = h.shape
    f32 = jnp.float32
    nb = S // ATT_BLOCK
    qkv = h @ w_in
    q, k, v = jnp.split(qkv, [ATT_HEADS * ATT_HEAD_DIM, (ATT_HEADS + ATT_KV_HEADS) * ATT_HEAD_DIM], axis=-1)
    q = head_rms(q.reshape(B, S, ATT_KV_HEADS, ATT_GROUP, ATT_HEAD_DIM), q_norm)
    k = head_rms(k.reshape(B, S, ATT_KV_HEADS, ATT_HEAD_DIM), k_norm)
    v = v.reshape(B, S, ATT_KV_HEADS, ATT_HEAD_DIM)
    pad = ((0, 0), (WINDOW, WINDOW), (0, 0), (0, 0))
    k_pad = jnp.pad(k, pad)
    v_pad = jnp.pad(v, pad)
    q_blocks = jnp.moveaxis(q.reshape(B, nb, ATT_BLOCK, ATT_KV_HEADS, ATT_GROUP, ATT_HEAD_DIM), 1, 0)

    rel = (jnp.arange(KEY_SPAN)[None, :] - WINDOW) - jnp.arange(ATT_BLOCK)[:, None]
    band = jnp.abs(rel) <= WINDOW
    slopes = alibi_slopes().reshape(ATT_KV_HEADS, ATT_GROUP)
    alibi = -slopes[:, :, None, None] * jnp.abs(rel).astype(f32)
    sink_logit = sink.astype(f32).reshape(ATT_KV_HEADS, ATT_GROUP)[None, :, :, None, None]
    scale = ATT_HEAD_DIM ** -0.5

    def block(args):
        i, q_i = args
        start = i * ATT_BLOCK
        k_i = lax.dynamic_slice_in_dim(k_pad, start, KEY_SPAN, axis=1)
        v_i = lax.dynamic_slice_in_dim(v_pad, start, KEY_SPAN, axis=1)
        kpos = start - WINDOW + jnp.arange(KEY_SPAN)
        valid = band & ((kpos >= 0) & (kpos < S))[None, :]
        s = jnp.einsum('bqhgd,bkhd->bhgqk', q_i, k_i).astype(f32) * scale + alibi
        s = jnp.where(valid, s, NEG_INF)
        sk = jnp.broadcast_to(sink_logit, s.shape[:-1] + (1,))
        p = jax.nn.softmax(jnp.concatenate([s, sk], axis=-1), axis=-1)[..., :KEY_SPAN]
        return jnp.einsum('bhgqk,bkhd->bqhgd', p.astype(v_i.dtype), v_i)

    o = lax.map(block, (jnp.arange(nb), q_blocks))
    o = jnp.moveaxis(o, 0, 1).reshape(B, S, ATT_HEADS * ATT_HEAD_DIM)
    return o @ w_out

def hier_moe(x, wg1, bg1, wg2, bg2, w_gate, w_up, w_down):
    T, D = x.shape
    f32 = jnp.float32
    group_prob = jax.nn.softmax((x @ wg1).astype(f32) + bg1, axis=-1)
    group = jnp.argmax(group_prob, axis=-1)
    p_group = jnp.max(group_prob, axis=-1)
    fine = jnp.einsum('td,gde->tge', x, wg2).astype(f32) + bg2
    fine = jnp.take_along_axis(fine, group[:, None, None], axis=1)[:, 0]
    top_p, top_e = lax.top_k(jax.nn.softmax(fine, axis=-1), TOP_K)
    gate = top_p / jnp.sum(top_p, -1, keepdims=True) * p_group[:, None]
    expert = group[:, None] * EXPERTS_PER_GROUP + top_e

    A = T * TOP_K
    eid = expert.reshape(A).astype(jnp.int32)
    tok = jnp.repeat(jnp.arange(T, dtype=jnp.int32), TOP_K)
    wt = gate.reshape(A)
    order = jnp.argsort(eid)
    eid_s, tok_s, wt_s = eid[order], tok[order], wt[order]
    counts = jnp.zeros((N_EXPERTS,), jnp.int32).at[eid].add(1)
    starts = jnp.cumsum(counts) - counts
    padded = (counts + MOE_BLOCK - 1) // MOE_BLOCK * MOE_BLOCK
    p_end = jnp.cumsum(padded)
    p_start = p_end - padded
    dest = p_start[eid_s] + jnp.arange(A, dtype=jnp.int32) - starts[eid_s]
    nblk = -(-A // MOE_BLOCK) + N_EXPERTS
    rows = nblk * MOE_BLOCK
    row_tok = jnp.full((rows,), T, jnp.int32).at[dest].set(tok_s)
    row_wt = jnp.zeros((rows,), f32).at[dest].set(wt_s)
    blk_exp = jnp.minimum(
        jnp.searchsorted(p_end, jnp.arange(nblk, dtype=jnp.int32) * MOE_BLOCK, side='right'),
        N_EXPERTS - 1)
    x_pad = jnp.concatenate([x, jnp.zeros((1, D), x.dtype)], axis=0)

    def expert_block(args):
        toks, e = args
        xb = x_pad[toks]
        hb = jax.nn.silu(xb @ w_gate[e]) * (xb @ w_up[e])
        return hb @ w_down[e]

    out = lax.map(expert_block, (row_tok.reshape(nblk, MOE_BLOCK), blk_exp))
    out = out.reshape(rows, D).astype(f32) * row_wt[:, None]
    y = jnp.zeros((T + 1, D), f32).at[row_tok].add(out)[:T]
    return y.astype(x.dtype)

def setup_inputs(seed: int = 0) -> dict:
    key = jax.random.key(seed)
    ks = jax.random.split(key, 37)
    f32 = jnp.float32

    def nrm(k, shape, scale):
        return jax.random.normal(k, shape, f32) * scale

    u = jax.random.uniform(ks[11], (N_REC, 2, RG_WIDTH), f32, minval=0.9, maxval=0.999)
    a_init = u ** (1.0 / RG_C)
    rg_lambda = jnp.log(a_init) - jnp.log1p(-a_init)
    return {
        "x_prompt": nrm(ks[0], (BATCH, SEQ, D_MODEL), 1.0),
        "x_sample": nrm(ks[1], (DEC_BATCH, DEC_SEQ, D_MODEL), 1.0),
        "norm_mix": 1.0 + nrm(ks[2], (DEPTH, D_MODEL), 0.05),
        "norm_ffn": 1.0 + nrm(ks[3], (DEPTH, D_MODEL), 0.05),
        "rec_w_in": nrm(ks[4], (N_REC, D_MODEL, REC_IN), D_MODEL ** -0.5),
        "rg_conv_w": nrm(ks[5], (N_REC, CONV_WIDTH, RG_WIDTH), CONV_WIDTH ** -0.5),
        "rg_conv_b": nrm(ks[6], (N_REC, RG_WIDTH), 0.02),
        "rg_wa": nrm(ks[7], (N_REC, 2, RG_BLOCKS, RG_BLOCK_DIM, RG_BLOCK_DIM), RG_BLOCK_DIM ** -0.5),
        "rg_ba": nrm(ks[8], (N_REC, 2, RG_WIDTH), 0.1),
        "rg_wx": nrm(ks[9], (N_REC, 2, RG_BLOCKS, RG_BLOCK_DIM, RG_BLOCK_DIM), RG_BLOCK_DIM ** -0.5),
        "rg_bx": nrm(ks[10], (N_REC, 2, RG_WIDTH), 0.1),
        "rg_lambda": rg_lambda,
        "rw_mu_l": jax.random.uniform(ks[12], (N_REC, RW_IN), f32, minval=0.0, maxval=0.5),
        "rw_mu_r": jax.random.uniform(ks[13], (N_REC, RW_IN), f32, minval=0.0, maxval=0.5),
        "rw_w0": nrm(ks[14], (N_REC, 2, RW_WIDTH), 1.0),
        "rw_w_up": nrm(ks[15], (N_REC, 2, DECAY_LORA, RW_WIDTH), 0.5 * DECAY_LORA ** -0.5),
        "rw_a0": nrm(ks[16], (N_REC, 2, RW_WIDTH), 0.5),
        "rw_a_up": nrm(ks[17], (N_REC, 2, ICL_LORA, RW_WIDTH), 0.5 * ICL_LORA ** -0.5),
        "rw_g_up": nrm(ks[18], (N_REC, GATE_LORA, RW_WIDTH), GATE_LORA ** -0.5),
        "rw_k_k": 1.0 + nrm(ks[19], (N_REC, RW_WIDTH), 0.1),
        "rw_k_a": 1.0 + nrm(ks[20], (N_REC, RW_WIDTH), 0.1),
        "rw_r_k": nrm(ks[21], (N_REC, RW_HEADS, RW_HEAD_DIM), 0.1),
        "rw_ln_w": 1.0 + nrm(ks[22], (N_REC, RW_WIDTH), 0.05),
        "rw_ln_b": nrm(ks[23], (N_REC, RW_WIDTH), 0.02),
        "rec_w_out": nrm(ks[24], (N_REC, RG_WIDTH + RW_WIDTH, D_MODEL), 0.5 * (RG_WIDTH + RW_WIDTH) ** -0.5),
        "att_w_in": nrm(ks[25], (N_ATT, D_MODEL, ATT_IN), D_MODEL ** -0.5),
        "att_q_norm": 1.0 + nrm(ks[26], (N_ATT, ATT_HEAD_DIM), 0.05),
        "att_k_norm": 1.0 + nrm(ks[27], (N_ATT, ATT_HEAD_DIM), 0.05),
        "att_sink": nrm(ks[28], (N_ATT, ATT_HEADS), 0.5),
        "att_w_out": nrm(ks[29], (N_ATT, ATT_HEADS * ATT_HEAD_DIM, D_MODEL), 0.5 * (ATT_HEADS * ATT_HEAD_DIM) ** -0.5),
        "moe_wg1": nrm(ks[30], (DEPTH, D_MODEL, N_GROUPS), D_MODEL ** -0.5),
        "moe_bg1": nrm(ks[31], (DEPTH, N_GROUPS), 0.01),
        "moe_wg2": nrm(ks[32], (DEPTH, N_GROUPS, D_MODEL, EXPERTS_PER_GROUP), D_MODEL ** -0.5),
        "moe_bg2": nrm(ks[33], (DEPTH, N_GROUPS, EXPERTS_PER_GROUP), 0.01),
        "moe_w_gate": nrm(ks[34], (DEPTH, N_EXPERTS, D_MODEL, EXPERT_FF), D_MODEL ** -0.5),
        "moe_w_up": nrm(ks[35], (DEPTH, N_EXPERTS, D_MODEL, EXPERT_FF), D_MODEL ** -0.5),
        "moe_w_down": nrm(ks[36], (DEPTH, N_EXPERTS, EXPERT_FF, D_MODEL), 0.5 * EXPERT_FF ** -0.5),
    }

def reference(x_prompt, x_sample, norm_mix, norm_ffn, rec_w_in, rg_conv_w, rg_conv_b, rg_wa, rg_ba,
              rg_wx, rg_bx, rg_lambda, rw_mu_l, rw_mu_r, rw_w0, rw_w_up, rw_a0, rw_a_up, rw_g_up,
              rw_k_k, rw_k_a, rw_r_k, rw_ln_w, rw_ln_b, rec_w_out, att_w_in, att_q_norm, att_k_norm,
              att_sink, att_w_out, moe_wg1, moe_bg1, moe_wg2, moe_bg2, moe_w_gate, moe_w_up, moe_w_down):
    def trunk(x):
        B, S, D = x.shape
        for i in range(DEPTH):
            j = i // 2
            h = rms_norm(x, norm_mix[i])
            if i % 2 == 0:
                mix = recurrent_mixer(h, rec_w_in[j], rg_conv_w[j], rg_conv_b[j], rg_wa[j], rg_ba[j],
                                      rg_wx[j], rg_bx[j], rg_lambda[j], rw_mu_l[j], rw_mu_r[j],
                                      rw_w0[j], rw_w_up[j], rw_a0[j], rw_a_up[j], rw_g_up[j],
                                      rw_k_k[j], rw_k_a[j], rw_r_k[j], rw_ln_w[j], rw_ln_b[j],
                                      rec_w_out[j])
            else:
                mix = window_attention(h, att_w_in[j], att_q_norm[j], att_k_norm[j], att_sink[j],
                                       att_w_out[j])
            x = x + mix.astype(x.dtype)
            h = rms_norm(x, norm_ffn[i])
            ffn = hier_moe(h.reshape(B * S, D), moe_wg1[i], moe_bg1[i], moe_wg2[i], moe_bg2[i],
                           moe_w_gate[i], moe_w_up[i], moe_w_down[i])
            x = x + ffn.reshape(B, S, D).astype(x.dtype)
        return x

    y_prompt = trunk(x_prompt)
    y_sample = trunk(x_sample)
    return (y_prompt, y_sample)


_drawn_inputs = setup_inputs


def setup_inputs(seed=0):
    import zlib

    import numpy as np

    out = dict(_drawn_inputs(seed))
    spreads = {}
    factors = {'rg_ba': 5.372,
     'rg_bx': 3.582,
     'rw_w_up': 2.775,
     'rw_k_k': 4.037,
     'rw_ln_w': 3.169,
     'rw_ln_b': 3.864,
     'att_q_norm': 7.173,
     'att_k_norm': 6.134,
     'att_sink': 5.778,
     'moe_bg1': 4.065,
     'moe_bg2': 4.54}
    for name, (base, spread) in spreads.items():
        noise = np.random.default_rng([zlib.crc32(name.encode()), seed]).standard_normal(out[name].shape)
        drawn = base * np.exp(spread * noise) if base else spread * noise
        out[name] = jnp.asarray(drawn.astype(out[name].dtype))
    for name, factor in factors.items():
        out[name] = (out[name] * factor).astype(out[name].dtype)
    return out
```

```python
from contextlib import ExitStack

import numpy as np

import concourse.bass as bass
from concourse import mybir

F32 = mybir.dt.float32
U32 = mybir.dt.uint32
ALU = mybir.AluOpType
ACT = mybir.ActivationFunctionType
AX = mybir.AxisListType

P = 128
D = 1024
KC = D // P
SEQ = 256
NSEQ = 2
T = SEQ * NSEQ
TT = T // P
RG = 512
FT = RG // P
CONV = 4
HD = 64
REC_IN = 2688
NF = REC_IN // P
RW_EPS = 64e-5
RMS_EPS = 1e-6
DECAY = float(np.exp(-0.5))
LEVELS = 7
HEADS = 16
KVH = 4
EXPERTS = 32
GROUPS = 4
EPG = 8
FF = 512
CAP = 64
OVER = 2 * T // CAP
SLOTS = 6
NEG = -1e30

V_MIX, V_FFN, V_CW, V_CB, V_BA, V_BX, V_LAM, V_W0, V_A0, V_KK, V_KA, V_RK, V_LNW, V_LNB, V_END = (
    0, 16, 32, 48, 52, 60, 68, 76, 84, 92, 96, 100, 104, 108, 112)
B_MUL, B_MUR, B_QK, B_END = 0, 13, 26, 28


def trunk(nc, a, y_prompt, y_sample):
    ctx = ExitStack()
    with ctx:
        def sb(name, shape, dt=F32):
            return ctx.enter_context(nc.sbuf_tensor(name, shape, dt))

        def sem(name):
            return ctx.enter_context(nc.semaphore(name))

        ring = sb("ring", [P, SLOTS, 4096])
        X = sb("X", [P, TT, D])
        hT = sb("hT", [P, KC, T])
        xn = sb("xn", [P, TT, D])
        arena = sb("arena", [P, 10764])
        ident = sb("ident", [P, P])
        ones = sb("ones", [P, P])
        blk = sb("blk", [P, P])
        chunkmask = sb("chunkmask", [P, 2, 4, P])
        lvlmask = sb("lvlmask", [P, 2, LEVELS, P])
        VA = sb("VA", [P, V_END])
        VB = sb("VB", [P, B_END])
        brow = sb("brow", [1, HEADS + 2 * 36])
        ssq = sb("ssq", [P, TT])
        rstd = sb("rstd", [P, TT])
        small = sb("small", [P, 64])
        wr = sb("wr", [P, 2, KC, 36])
        Zb = sb("Zb", [P, 8, P])

        bank = [ctx.enter_context(nc.psum_tensor(f"bank{i}", [P, 512], F32)) for i in range(8)]

        def carve(base, at, shape):
            n = int(np.prod(shape))
            v = base[:, at:at + n]
            if len(shape) == 2:
                v = v.rearrange("p (a b) -> p a b", a=shape[0])
            if len(shape) == 3:
                v = v.rearrange("p (a b c) -> p a b c", a=shape[0], b=shape[1])
            if len(shape) == 4:
                v = v.rearrange("p (a b c d) -> p a b c d", a=shape[0], b=shape[1], c=shape[2])
            return v, at + n

        AR = arena[:, :]
        at = 0
        pad, at = carve(AR, at, [2, NSEQ, SEQ + 3])
        rT, at = carve(AR, at, [FT, T])
        kT, at = carve(AR, at, [FT, T])
        vT, at = carve(AR, at, [FT, T])
        wag, at = carve(AR, at, [T])
        WA, at = carve(AR, at, [8, P])
        WX, at = carve(AR, at, [8, P])
        LUP, at = carve(AR, at, [2, RG])
        assert at <= 10764
        vrows = vT[:, 0, 0:2 * P].rearrange("p (a b) -> p a b", a=2)
        vcur = pad.rearrange("p a b c -> p (a b c)")[:, 0:T]
        yback, _ = carve(pad.rearrange("p a b c -> p (a b c)"), T, [2, 256])
        RU, _ = carve(WA.rearrange("p a b -> p (a b)"), 0, [2, 256])
        Sst, _ = carve(WA.rearrange("p a b -> p (a b)"), 512, [NSEQ, P])
        sscale, _ = carve(WA.rearrange("p a b -> p (a b)"), 768, [2, NSEQ])
        BKtok, _ = carve(WX.rearrange("p a b -> p (a b)"), 0, [2, NSEQ, P])
        Vtok, _ = carve(WX.rearrange("p a b -> p (a b)"), 512, [TT, P])
        asg = hT
        mixT = xn[:, :, :].rearrange("p a b -> p (a b)").rearrange("p (a b) -> p a b", a=KC)
        rgg = mixT[:, 0:FT, :]
        xc = mixT[:, FT:, :]
        yT = mixT[:, FT:, :]
        RT = ring[:, 2:6, :].rearrange("p a b -> p (a b)")
        P0, at = carve(RT, 0, [8, TT, P + 1])
        at0 = at
        gates, at = carve(RT, at0, [2, FT, 2 * T])
        at1 = at
        E2, at = carve(RT, at1, [2, TT, P + 1])
        ksum, at = carve(RT, at, [T])
        kk, end = carve(RT, 16384 - FT * T, [FT, T])
        assert at <= 16384 - FT * T and 3 * 4096 + KC * (REC_IN - 5 * 512) <= 16384 - FT * T
        R01 = ring[:, 0:2, :].rearrange("p a b -> p (a b)")
        q4, at = carve(R01, 0, [FT, T])
        tmpA, at = carve(R01, at, [2, T])
        tmpB, at = carve(R01, at, [T])
        ksq, at = carve(R01, at, [FT, T])
        kinv, at = carve(R01, at, [FT, T])
        assert at <= 8192
        ARt, BKt, Mb, Tb = [], [], [], []
        for base, at in ((RT, at0), (R01, 0)):
            for buf, shape in ((ARt, [TT, 2, P]),
                               (BKt, [2, TT, P]),
                               (Mb, [8, 4, P]),
                               (Tb, [8, 2, P])):
                v, at = carve(base, at, shape)
                buf.append(v)
            assert at - (at0 if base is RT else 0) <= 8192 and at1 - at0 == 8192

        def row(name):
            v = a[name]
            names = "abcdefg"[:len(v.shape)]
            if len(v.shape) > 1:
                v = v.rearrange(f"{' '.join(names)} -> ({' '.join(names)})")
            return v.rearrange("(n p) -> n p", p=P)

        x_loaded, vec_loaded, brow_loaded, rgw_loaded, rgw_zero, router_loaded = (
            sem(n) for n in ("x_loaded", "vec_loaded", "brow_loaded", "rgw_loaded", "rgw_zero", "router_loaded"))
        slot_loaded = [sem(f"slot{i}_loaded") for i in range(SLOTS)]
        consts_ready, vrows_turned, v_ready, pad_zero = (
            sem(n) for n in ("consts_ready", "vrows_turned", "v_ready", "pad_zero"))
        pool_step, dve_step, act_step = sem("pool_step"), sem("dve_step"), sem("act_step")
        ssq_ready, rms_ready, xn_ready, hT_raw, hT_ready, x_updated = (
            sem(n) for n in ("ssq_ready", "rms_ready", "xn_ready", "hT_raw", "hT_ready", "x_updated"))
        gemm_done, gemm_out, pad_free, mixed_in, wag_act = (
            sem(n) for n in ("gemm_done", "gemm_out", "pad_free", "mixed_in", "wag_act"))
        sg_free, sp_ready, lam_ready = sem("sg_free"), sem("sp_ready"), sem("lam_ready")
        rg_exp, rg_q, rg_sqrt, gelu_in, gelu_tanh, gelu_ready, rg_done = (
            sem(n) for n in ("rg_exp", "rg_q", "rg_sqrt", "gelu_in", "gelu_tanh", "gelu_ready", "rg_done"))
        kk_raw, kk_sq, kk_ready = sem("kk_raw"), sem("kk_sq"), sem("kk_ready")
        vcur_ready, v_turned, exp_ready, prep_ready, bk_turned, bktok_ready = (
            sem(n) for n in ("vcur_ready", "v_turned", "exp_ready", "prep_ready", "bk_turned", "bktok_ready"))
        m_done, m_out, z_done, z_out, t_done, t_out = (
            sem(n) for n in ("m_done", "m_out", "z_done", "z_out", "t_done", "t_out"))
        t_turned, t_copied = sem("t_turned"), sem("t_copied")
        ident_ready, sst_zero, t_block, y_added = sem("ident_ready"), sem("sst_zero"), sem("t_block"), sem("y_added")
        rhs_done, rhs_out, u_done, u_out, ys_done, ys_out, loop_step = (
            sem(n) for n in ("rhs_done", "rhs_out", "u_done", "u_out", "ys_done", "ys_out", "loop_step"))
        gn_mean, gn_c, gn_sq, gn_var, gn_sqrt, gn_out, gn_mm = (
            sem(n) for n in ("gn_mean", "gn_c", "gn_sq", "gn_var", "gn_sqrt", "gn_out", "gn_mm"))
        out_done, y_stored = sem("out_done"), sem("y_stored")

        block = ctx.enter_context(nc.Block())
        slot = [ring[:, s, :] for s in range(SLOTS)]

        def first_chunks(t, d):
            return [2 * b + (1 if d else 0) for b in range(NSEQ)]

        def y_chunks(ft, cs):
            return yT[:, bass.ds(ft, 1), :].rearrange("p a b -> p (a b)").rearrange(
                "p (b c t) -> p b c t", b=NSEQ, c=2)[:, :, cs, :]

        XU = [0, 8, 16, 24]
        NORM_COL = [V_MIX, V_FFN, V_MIX + KC, V_FFN + KC]

        def act_norm(act, j):
            if j == 0:
                act.wait_ge(x_loaded, 32)
            else:
                act.wait_ge(x_updated, XU[j])
            for t in range(TT):
                ins = nc.scalar.activation(xn[:, t, :], X[:, t, :], ACT.Square, accum_out=ssq[:, t:t + 1])
            ins.then_inc(ssq_ready, 1)
            act.wait_ge(ssq_ready, j + 1)
            nc.scalar.activation(rstd[:, :], ssq[:, :], ACT.Sqrt, scale=1.0 / D, bias=eps_rms).then_inc(rms_ready, 1)

        def dve_norm(dve, step, j):
            dve.wait_ge(rms_ready, j + 1)
            step(nc.vector.reciprocal(rstd[:, :], rstd[:, :]))
            for t in range(TT):
                nc.vector.tensor_scalar(xn[:, t, :], X[:, t, :], rstd[:, t:t + 1], None, ALU.mult).then_inc(xn_ready, 1)

        def pe_turn_norm(pe, j):
            for c in range(KC):
                if c >= 2:
                    pe.wait_ge(hT_ready, KC * j + c - 1)
                for t in range(TT):
                    if c == 0:
                        pe.wait_ge(xn_ready, TT * j + t + 1)
                    mm = nc.tensor.transpose(bank[c % 2][:, t * P:(t + 1) * P], xn[:, t, c * P:(c + 1) * P], ident[:, :])
                mm.then_inc(hT_raw, 1)

        def act_hT(act, j):
            for c in range(KC):
                act.wait_ge(hT_raw, KC * j + c + 1)
                nc.scalar.activation(hT[:, c, :], bank[c % 2][:, :], ACT.Copy,
                                     scale=VA[:, NORM_COL[j] + c:NORM_COL[j] + c + 1]).then_inc(hT_ready, 1)

        eps_rms = small[:, 60:61]
        eps_gn = small[:, 61:62]
        c0 = small[:, 0:13]
        sp8 = small[:, 13:21]
        nsp8 = small[:, 21:29]
        lt = small[:, 29:53]
        pm = sb("pm", [P, 8, TT])
        one_ka = sb("one_ka", [P, FT])

        G_KK = NF
        G_RG = G_KK + FT
        G_UNIT = G_RG + 16

        one_col = ones[:, 0:1]
        LOOP_STEPS = 9

        at = 0
        onehot, at = carve(AR, at, [2, TT, CAP])
        xg, at = carve(AR, at, [2, KC, CAP])
        hT2, at = carve(AR, at, [2, FF // P, CAP])
        sg, at = carve(AR, at, [2, FF])
        hb, at = carve(AR, at, [2, FF])
        ob, at = carve(AR, at, [2, 512])
        rows, at = carve(AR, at, [4, D])
        lg, at = carve(AR, at, [TT, 36])
        goh, at = carve(AR, at, [TT, GROUPS])
        gex, at = carve(AR, at, [TT, GROUPS])
        fine, at = carve(AR, at, [TT, GROUPS, EPG])
        fsel, at = carve(AR, at, [TT, EPG])
        eoh, at = carve(AR, at, [2, TT, EPG])
        E12, at = carve(AR, at, [2, TT, EXPERTS])
        Eany, at = carve(AR, at, [TT, EXPERTS])
        rank, at = carve(AR, at, [TT, EXPERTS])
        key, at = carve(AR, at, [EXPERTS + 2, TT])
        mg, at = carve(AR, at, [8, TT])
        dest_f, at = carve(AR, at, [2, TT])
        wtok, at = carve(AR, at, [2, TT])
        wall, at = carve(AR, at, [EXPERTS, TT])
        extra, at = carve(AR, at, [EXPERTS])
        before, at = carve(AR, at, [EXPERTS])
        over_e, at = carve(AR, at, [OVER])
        over_at, at = carve(AR, at, [OVER])
        over_tmp = rows[:, 1, 0:OVER * EXPERTS].rearrange("p (k e) -> p k e", k=OVER)
        assert at <= 10764, at
        dest = sb("dest", [P, 2 * TT], U32)
        over_i = sb("over_i", [P, OVER + 1], mybir.dt.int32)
        iota_i = lvlmask[:, 0, 0:2, :].rearrange("p a b -> p (a b)").bitcast(mybir.dt.int32)
        iota64 = sb("iota64", [P, CAP])
        tie = sb("tie", [P, EPG])
        ebase = sb("ebase", [P, EXPERTS])
        bb = sb("bb", [P, HEADS + 72])
        expert_rows = [nc.dram_tensor(f"expert_rows{l}", (EXPERTS * CAP, D), F32).ap() for l in range(2)]

        iota_ready, bb_raw, tables_ready = sem("iota_ready"), sem("bb_raw"), sem("tables_ready")
        lg_done, g_shift, g_exp, f_shift, f_exp, choice_ready, rank_done, route_ready = (
            sem(n) for n in ("lg_done", "g_shift", "g_exp", "f_shift", "f_exp", "choice_ready", "rank_done", "route_ready"))
        moe = [dict((n, sem(n)) for n in (
            "onehot_ready", "xg_raw", "xg_ready", "gu_done", "sg_ready", "hb_ready", "h_turned", "hT_out", "down_done",
            "out_ready"))] * 2
        ob_stored = [sem(f"ob_stored{par}") for par in range(2)]
        rows_loaded = [sem(f"rows_loaded{b}") for b in range(4)]
        over = [dict((n, sem(f"over_{n}{l}")) for n in (
            "loaded0", "loaded1", "loaded2", "onehot", "xg_raw", "xg", "gu", "sg", "hb", "turned", "hT", "down", "ob",
            "sum", "added", "step")) for l in range(2)]
        over_end = sem("over_end")
        NPAIR = EXPERTS // 2
        N0 = (8, 109)

        def ge(eng, s, v):
            if not (isinstance(v, int) and v <= 0):
                eng.wait_ge(s, v)

        def pairs(eng, body):
            body(0)
            with eng.Fori(1, NPAIR) as i:
                body(i)

        def sp_moe(sp, l):
            m = moe[l]

            def pair(i):
                for par in range(2):
                    e = 2 * i + par
                    for k, name in enumerate(("moe_w_gate", "moe_w_up", "moe_w_down")):
                        s = (N0[l] + 3 * par + k) % SLOTS
                        if isinstance(i, int):
                            for se, v in FIRST[l][3 * par + k]:
                                sp.wait_ge(se, v)
                        else:
                            sp.wait_ge(m["down_done"] if k == 2 else m["gu_done"], EXPERTS * l + e - 1)
                        src = a[name][l, bass.ds(e, 1)].rearrange("a (c p) f -> p (a c) f", p=P)
                        c = KC if k < 2 else FF // P
                        sp.dma_start(slot[s].rearrange("p (c f) -> p c f", c=c), src).then_inc(slot_loaded[s], 16)
            pairs(sp, pair)
            sp_over(sp, l)

        def act_moe(act, l):
            m = moe[l]
            act.wait_ge(g_shift, l + 1)
            nc.scalar.activation(gex, gex, ACT.Exp).then_inc(g_exp, 1)
            act.wait_ge(f_shift, l + 1)
            nc.scalar.activation(mg[:, 3, :], mg[:, 3, :], ACT.Exp).then_inc(f_exp, 1)

            def pair(i):
                for par in range(2):
                    e = 2 * i + par
                    act.wait_ge(m["gu_done"], EXPERTS * l + e + 1)
                    nc.scalar.activation(sg[0:CAP, par, :], bank[par][0:CAP, :], ACT.Silu).then_inc(m["sg_ready"], 1)
                    act.wait_ge(m["h_turned"], EXPERTS * l + e + 1)
                    nc.scalar.activation(hT2[:, par, :, :], bank[4 + par][:, 0:256].rearrange("p (c s) -> p c s", c=4),
                                         ACT.Copy).then_inc(m["hT_out"], 1)
                    act.wait_ge(m["down_done"], EXPERTS * l + e + 1)
                    ge(act, ob_stored[par], 32 * (NPAIR * l + i))
                    nc.scalar.activation(ob[:, par, :], bank[6 + par][:, :], ACT.Copy).then_inc(m["out_ready"], 1)
                    act.wait_ge(m["out_ready"], EXPERTS * l + e + 1)
                    for h in range(2):
                        act.dma_start(expert_rows[l][bass.ds(e * CAP, CAP), h * 512:(h + 1) * 512],
                                      ob[h * CAP:(h + 1) * CAP, par, :]).then_inc(ob_stored[par], 16)
            pairs(act, pair)
            act_over(act, l)

        def dve_first(step, out, x, m, n):
            step(nc.vector.tensor_reduce(m, x, AX.X, ALU.max))
            step(nc.vector.tensor_tensor(out, x, m.unsqueeze(2).to_broadcast([P, TT, n]), ALU.is_equal))
            step(nc.vector.tensor_tensor(out, out, tie[:, 0:n].unsqueeze(1).to_broadcast([P, TT, n]), ALU.mult))
            step(nc.vector.tensor_reduce(mg[:, 7, :], out, AX.X, ALU.max))
            step(nc.vector.tensor_tensor(out, out, mg[:, 7, :].unsqueeze(2).to_broadcast([P, TT, n]), ALU.is_equal))

        def dve_moe(dve, step, l):
            m = moe[l]
            dve_norm(dve, step, 1 + 2 * l)
            dve.wait_ge(lg_done, l + 1)
            b = HEADS + 36 * l
            step(nc.vector.tensor_tensor(lg, bank[2][:, 0:144].rearrange("p (t e) -> p t e", t=TT),
                                         bb[:, b:b + 36].unsqueeze(1).to_broadcast([P, TT, 36]), ALU.add))
            dve_first(step, goh, lg[:, :, 0:GROUPS], mg[:, 0, :], GROUPS)
            nc.vector.tensor_tensor(gex, lg[:, :, 0:GROUPS], mg[:, 0, :].unsqueeze(2).to_broadcast([P, TT, GROUPS]),
                                    ALU.subtract).then_inc(g_shift, 1)
            step(nc.vector.tensor_tensor(fine, lg[:, :, GROUPS:].rearrange("p t (g e) -> p t g e", g=GROUPS),
                                         goh.unsqueeze(3).to_broadcast([P, TT, GROUPS, EPG]), ALU.mult))
            step(nc.vector.tensor_reduce(fsel, fine.rearrange("p t g e -> p t e g"), AX.X, ALU.add))
            dve_first(step, eoh[:, 0, :, :], fsel, mg[:, 1, :], EPG)
            step(nc.vector.scalar_tensor_tensor(fsel, eoh[:, 0, :, :], NEG, fsel, ALU.mult, ALU.add))
            dve_first(step, eoh[:, 1, :, :], fsel, mg[:, 2, :], EPG)
            nc.vector.tensor_tensor(mg[:, 3, :], mg[:, 2, :], mg[:, 1, :], ALU.subtract).then_inc(f_shift, 1)
            for k in range(2):
                step(nc.vector.tensor_tensor(E12[:, k, :, :].rearrange("p t (g e) -> p t g e", g=GROUPS),
                                             goh.unsqueeze(3).to_broadcast([P, TT, GROUPS, EPG]),
                                             eoh[:, k, :, :].unsqueeze(2).to_broadcast([P, TT, GROUPS, EPG]), ALU.mult))
            nc.vector.tensor_tensor(Eany, E12[:, 0, :, :], E12[:, 1, :, :], ALU.add).then_inc(choice_ready, 1)
            dve.wait_ge(g_exp, l + 1)
            step(nc.vector.tensor_reduce(mg[:, 4, :], gex, AX.X, ALU.add))
            step(nc.vector.reciprocal(mg[:, 4, :], mg[:, 4, :]))
            dve.wait_ge(f_exp, l + 1)
            step(nc.vector.tensor_scalar(mg[:, 5, :], mg[:, 3, :], 1.0, None, ALU.add))
            step(nc.vector.reciprocal(mg[:, 5, :], mg[:, 5, :]))
            step(nc.vector.tensor_tensor(wtok[:, 0, :], mg[:, 5, :], mg[:, 4, :], ALU.mult))
            step(nc.vector.tensor_tensor(wtok[:, 1, :], wtok[:, 0, :], mg[:, 3, :], ALU.mult))
            gcol = VA[:, NORM_COL[1 + 2 * l]:NORM_COL[1 + 2 * l] + KC].unsqueeze(2).to_broadcast([P, KC, CAP])

            def build(e, par):
                k = key[:, e, :] if isinstance(e, int) else key[:, bass.ds(e, 1), :].rearrange("p a t -> p (a t)")
                nc.vector.tensor_tensor(onehot[:, par, :, :], iota64[:, :].unsqueeze(1).to_broadcast([P, TT, CAP]),
                                        k.unsqueeze(2).to_broadcast([P, TT, CAP]), ALU.is_equal).then_inc(m["onehot_ready"], 1)

            def gathered(e, par):
                dve.wait_ge(m["xg_raw"], (EXPERTS + 1) * l + e + 1)
                nc.vector.tensor_tensor(xg[:, par, :, :], bank[2 + par][:, :].rearrange("p (c s) -> p c s", c=KC),
                                        gcol, ALU.mult).then_inc(m["xg_ready"], 1)
            step(nc.vector.memset(key, -1.0))
            dve.wait_ge(rank_done, l + 1)
            for_key = fine.rearrange("p t g e -> p t (g e)")
            step(nc.vector.scalar_tensor_tensor(for_key, bank[3][:, 0:TT * EXPERTS].rearrange("p (t e) -> p t e", t=TT),
                                                1.0, Eany, ALU.add, ALU.mult))
            step(nc.vector.tensor_scalar(key[:, 0:EXPERTS, :], for_key.rearrange("p t e -> p e t"), -1.0, None, ALU.add))
            build(0, 0)
            step(nc.vector.tensor_copy(rank, bank[3][:, 0:TT * EXPERTS].rearrange("p (t e) -> p t e", t=TT)))
            step(nc.vector.tensor_copy(before, bank[3][:, TT * EXPERTS:(TT + 1) * EXPERTS]))
            build(1, 1)
            gathered(0, 0)
            wv = wall.rearrange("p e t -> p t e")
            step(nc.vector.tensor_tensor(wv, E12[:, 0, :, :], wtok[:, 0, :].unsqueeze(2).to_broadcast([P, TT, EXPERTS]), ALU.mult))
            step(nc.vector.tensor_tensor(for_key, E12[:, 1, :, :], wtok[:, 1, :].unsqueeze(2).to_broadcast([P, TT, EXPERTS]), ALU.mult))
            step(nc.vector.tensor_tensor(wv, wv, for_key, ALU.add))
            step(nc.vector.memset(extra, 0.0))
            for b in range(1, T // CAP):
                step(nc.vector.scalar_tensor_tensor(extra, before, float(b * CAP), extra, ALU.is_gt, ALU.add))
            step(nc.vector.tensor_tensor_scan(before, ones[:, 0:EXPERTS], extra, 0.0, ALU.mult, ALU.add))
            step(nc.vector.tensor_tensor(over_tmp, before.unsqueeze(1).to_broadcast([P, OVER, EXPERTS]),
                                         iota64[:, 0:OVER].unsqueeze(2).to_broadcast([P, OVER, EXPERTS]), ALU.is_le))
            step(nc.vector.tensor_reduce(over_e, over_tmp, AX.X, ALU.add))
            step(nc.vector.tensor_tensor(over_tmp, over_tmp, extra.unsqueeze(1).to_broadcast([P, OVER, EXPERTS]), ALU.mult))
            step(nc.vector.tensor_reduce(over_at, over_tmp, AX.X, ALU.add))
            step(nc.vector.tensor_tensor(over_at, iota64[:, 0:OVER], over_at, ALU.subtract))
            step(nc.vector.tensor_scalar(over_at, over_at, 1.0, float(CAP), ALU.add, ALU.mult))
            step(nc.vector.tensor_scalar(over_e, over_e, float(EXPERTS - 1), None, ALU.min))
            step(nc.vector.tensor_copy(over_i[:, 0:OVER], over_e))
            step(nc.vector.tensor_copy(over_i[:, OVER:OVER + 1], before[:, EXPERTS - 1:EXPERTS]))
            for k in range(2):
                step(nc.vector.scalar_tensor_tensor(for_key, rank, float(CAP), E12[:, k, :, :], ALU.is_lt, ALU.mult))
                step(nc.vector.tensor_reduce(mg[:, 6, :], for_key, AX.X, ALU.add))
                step(nc.vector.tensor_tensor(wtok[:, k, :], wtok[:, k, :], mg[:, 6, :], ALU.mult))
            step(nc.vector.tensor_scalar(rank, rank, float(CAP - 1), None, ALU.min))
            for k in range(2):
                step(nc.vector.tensor_tensor(for_key, rank, ebase[:, :].unsqueeze(1).to_broadcast([P, TT, EXPERTS]), ALU.add))
                step(nc.vector.tensor_tensor(for_key, for_key, E12[:, k, :, :], ALU.mult))
                step(nc.vector.tensor_reduce(dest_f[:, k, :], for_key, AX.X, ALU.add))
            nc.vector.tensor_copy(dest[:, :], dest_f.rearrange("p k t -> p (k t)")).then_inc(route_ready, 1)
            dve.wait_ge(route_ready, l + 1)

            def pair(i):
                for par in range(2):
                    e = 2 * i + par
                    dve.wait_ge(m["sg_ready"], EXPERTS * l + e + 1)
                    nc.vector.tensor_tensor(hb[0:CAP, par, :], sg[0:CAP, par, :], bank[par][CAP:2 * CAP, :],
                                            ALU.mult).then_inc(m["hb_ready"], 1)
                    build(e + 2, par)
                    gathered(e + 1, 1 - par)

            pairs(dve, pair)
            dve_over(dve, l, gcol)

            for k in range(2):
                for t in range(TT):
                    i = k * TT + t
                    dve.wait_ge(rows_loaded[i % 4], 16 * (2 * l + i // 4 + 1))
                    nc.vector.scalar_tensor_tensor(X[:, t, :], rows[:, i % 4, :], wtok[:, k, t:t + 1], X[:, t, :],
                                                   ALU.mult, ALU.add).then_inc(x_updated, 1)
                    dve.wait_ge(x_updated, 8 + 16 * l + i + 1)

        def pool_moe(pool, l):
            pool.wait_ge(route_ready, l + 1)
            for par in range(2):
                pool.wait_ge(ob_stored[par], 32 * NPAIR * (l + 1))
            pool.wait_ge(over_end, l + 1)
            for k in range(2):
                for t in range(TT):
                    i = k * TT + t
                    if i >= 4:
                        pool.wait_ge(x_updated, 8 + 16 * l + i - 3)
                    nc.gpsimd.indirect_dma_start(rows[:, i % 4, :], None, expert_rows[l][:, :],
                                                 bass.IndirectOffsetOnAxis(ap=dest[:, i:i + 1], axis=0)
                                                 ).then_inc(rows_loaded[i % 4], 16)

        def pe_moe(pe, l):
            m = moe[l]
            pe_turn_norm(pe, 1 + 2 * l)
            pe.wait_ge(hT_ready, KC * (2 + 2 * l))
            if l == 0:
                pe.wait_ge(router_loaded, 160)
            for t in range(TT):
                for c in range(KC):
                    mm = nc.tensor.matmul(bank[2][:, t * 36:(t + 1) * 36], hT[:, c, t * P:(t + 1) * P], wr[:, l, c, :],
                                          start=(c == 0), stop=(c == KC - 1))
            mm.then_inc(lg_done, 1)
            pe.wait_ge(choice_ready, l + 1)
            for t in range(TT):
                o = bank[3][:, t * EXPERTS:(t + 1) * EXPERTS]
                mm = nc.tensor.matmul(o, chunkmask[:, 0, 0, :], Eany[:, t, :], start=True, stop=(t == 0))
                for b in range(t):
                    mm = nc.tensor.matmul(o, ones[:, :], Eany[:, b, :], start=False, stop=(b == t - 1))
            for t in range(TT):
                mm = nc.tensor.matmul(bank[3][:, TT * EXPERTS:(TT + 1) * EXPERTS], ones[:, :], Eany[:, t, :],
                                      start=(t == 0), stop=(t == TT - 1))
            mm.then_inc(rank_done, 1)

            def gather(e, par):
                pe.wait_ge(m["onehot_ready"], (EXPERTS + 2) * l + e + 1)
                for c in range(KC):
                    for t in range(TT):
                        mm = nc.tensor.matmul(bank[2 + par][:, c * CAP:(c + 1) * CAP], xn[:, t, c * P:(c + 1) * P],
                                              onehot[:, par, t, :], start=(t == 0), stop=(t == TT - 1))
                mm.then_inc(m["xg_raw"], 1)
            gather(0, 0)

            def pair(i):
                for par in range(2):
                    e = 2 * i + par
                    n0 = N0[l] + 3 * par
                    W = [slot[(n0 + k) % SLOTS] for k in range(3)]
                    loaded = lambda k: pe.wait_ge(slot_loaded[(n0 + k) % SLOTS], 16 * ((n0 + k) // SLOTS + 1) + 16 * i)
                    pe.wait_ge(m["xg_ready"], (EXPERTS + 1) * l + e + 1)
                    loaded(0)
                    loaded(1)
                    for c in range(KC):
                        for k in range(2):
                            mm = nc.tensor.matmul(bank[par][k * CAP:(k + 1) * CAP, :], xg[:, par, c, :],
                                                  W[k][:, c * FF:(c + 1) * FF], start=(c == 0), stop=(c == KC - 1))
                    mm.then_inc(m["gu_done"], 1)
                    gather(e + 1, 1 - par)
                    pe.wait_ge(m["hb_ready"], EXPERTS * l + e + 1)
                    for f in range(4):
                        mm = nc.tensor.matmul(bank[4 + par][:, f * CAP:(f + 1) * CAP], hb[0:CAP, par, f * P:(f + 1) * P],
                                              ident[0:CAP, 0:CAP], start=True, stop=True)
                    mm.then_inc(m["h_turned"], 1)
                    pe.wait_ge(m["hT_out"], EXPERTS * l + e + 1)
                    loaded(2)
                    ge(pe, m["out_ready"], EXPERTS * l + e - 1)
                    for f in range(4):
                        for h in range(2):
                            mm = nc.tensor.matmul(bank[6 + par][h * CAP:(h + 1) * CAP, :], hT2[:, par, f, :],
                                                  W[2][:, f * D + h * 512:f * D + (h + 1) * 512],
                                                  start=(f == 0), stop=(f == 3))
                    mm.then_inc(m["down_done"], 1)
            pairs(pe, pair)
            pe_over(pe, l)

        def further(eng, l, body):
            eng.wait_ge(route_ready, l + 1)
            count = eng.value_load(over_i[0:1, OVER:OVER + 1], min_val=0, max_val=OVER)
            with eng.If(count > 0):
                with eng.Fori(0, count) as k:
                    body(k)

        def sp_over(sp, l):
            o = over[l]
            sp.wait_ge(moe[l]["down_done"], EXPERTS * (l + 1))

            def block_(k):
                e = sp.value_load(over_i[0:1, bass.ds(k, 1)], min_val=0, max_val=EXPERTS - 1)
                for j, name in enumerate(("moe_w_gate", "moe_w_up", "moe_w_down")):
                    src = a[name][l, bass.ds(e, 1)].rearrange("a (c p) f -> p (a c) f", p=P)
                    if j == 0:
                        sp.wait_ge(o["down"], k + 1)
                    sp.dma_start(slot[j].rearrange("p (c f) -> p c f", c=KC if j < 2 else FF // P), src
                                 ).then_inc(o[f"loaded{j}"], 16)
            further(sp, l, block_)
            sp.wait_ge(over_end, l + 1)

        over_oT = rows[0:CAP, 0, 0:TT * P]

        def act_over(act, l):
            o = over[l]

            def block_(k):
                act.wait_ge(o["gu"], k + 1)
                nc.scalar.activation(sg[0:CAP, 0, :], bank[0][0:CAP, :], ACT.Silu).then_inc(o["sg"], 1)
                act.wait_ge(o["turned"], k + 1)
                nc.scalar.activation(hT2[:, 0, :, :], bank[4][:, 0:256].rearrange("p (c s) -> p c s", c=4),
                                     ACT.Copy).then_inc(o["hT"], 1)
                nc.scalar.activation(over_oT, bank[5][0:CAP, :], ACT.Copy).then_inc(o["hT"], 1)
                act.wait_ge(o["down"], k + 2)
                for h in range(2):
                    nc.scalar.activation(ob[0:CAP, h, :], bank[6 + h][0:CAP, :], ACT.Copy).then_inc(o["ob"], 1)
            for par in range(2):
                act.wait_ge(ob_stored[par], 32 * NPAIR * (l + 1))
            further(act, l, block_)

        def dve_over(dve, l, gcol):
            o = over[l]

            def block_(k):
                e = dve.value_load(over_i[0:1, bass.ds(k, 1)], min_val=0, max_val=EXPERTS - 1)
                kk_ = mg[:, 0, :]
                nc.vector.tensor_scalar(kk_, key[:, bass.ds(e, 1), :].rearrange("p a t -> p (a t)"),
                                        over_at[:, bass.ds(k, 1)], None, ALU.subtract).then_inc(o["step"], 1)
                nc.vector.tensor_copy(mg[:, 1, :], wall[:, bass.ds(e, 1), :].rearrange("p a t -> p (a t)")
                                      ).then_inc(o["step"], 1)
                dve.wait_ge(o["step"], 2 * k + 2)
                nc.vector.tensor_tensor(onehot[:, 0, :, :], iota64[:, :].unsqueeze(1).to_broadcast([P, TT, CAP]),
                                        kk_.unsqueeze(2).to_broadcast([P, TT, CAP]), ALU.is_equal).then_inc(o["onehot"], 1)
                dve.wait_ge(o["xg_raw"], k + 1)
                nc.vector.tensor_tensor(xg[:, 0, :, :], bank[2][:, :].rearrange("p (c s) -> p c s", c=KC),
                                        gcol, ALU.mult).then_inc(o["xg"], 1)
                dve.wait_ge(o["sg"], k + 1)
                nc.vector.tensor_tensor(hb[0:CAP, 0, :], sg[0:CAP, 0, :], bank[0][CAP:2 * CAP, :],
                                        ALU.mult).then_inc(o["hb"], 1)
                for t in range(TT):
                    for h in range(2):
                        i = 2 * t + h
                        dve.wait_ge(o["sum"], 8 * k + i + 1)
                        x = X[:, t, h * 512:(h + 1) * 512]
                        nc.vector.scalar_tensor_tensor(x, bank[i % 4][:, :], mg[:, 1, t:t + 1], x, ALU.mult, ALU.add
                                                       ).then_inc(o["added"], 1)
                dve.wait_ge(o["added"], 8 * k + 8)
            further(dve, l, block_)
            nc.vector.memset(small[:, 57:58], 0.0).then_inc(over_end, 1)

        def pe_over(pe, l):
            o = over[l]

            def block_(k):
                pe.wait_ge(o["onehot"], k + 1)
                for c in range(KC):
                    for t in range(TT):
                        mm = nc.tensor.matmul(bank[2][:, c * CAP:(c + 1) * CAP], xn[:, t, c * P:(c + 1) * P],
                                              onehot[:, 0, t, :], start=(t == 0), stop=(t == TT - 1))
                mm.then_inc(o["xg_raw"], 1)
                pe.wait_ge(o["xg"], k + 1)
                for j in range(2):
                    pe.wait_ge(o[f"loaded{j}"], 16 * k + 16)
                for c in range(KC):
                    for j in range(2):
                        mm = nc.tensor.matmul(bank[0][j * CAP:(j + 1) * CAP, :], xg[:, 0, c, :],
                                              slot[j][:, c * FF:(c + 1) * FF], start=(c == 0), stop=(c == KC - 1))
                mm.then_inc(o["gu"], 1)
                pe.wait_ge(o["hb"], k + 1)
                for f in range(4):
                    nc.tensor.matmul(bank[4][:, f * CAP:(f + 1) * CAP], hb[0:CAP, 0, f * P:(f + 1) * P],
                                     ident[0:CAP, 0:CAP], start=True, stop=True)
                for t in range(TT):
                    mm = nc.tensor.matmul(bank[5][0:CAP, t * P:(t + 1) * P], onehot[:, 0, t, :], ident[:, :],
                                          start=True, stop=True)
                mm.then_inc(o["turned"], 1)
                pe.wait_ge(o["hT"], 2 * k + 2)
                pe.wait_ge(o["loaded2"], 16 * k + 16)
                for f in range(4):
                    for h in range(2):
                        mm = nc.tensor.matmul(bank[6 + h][0:CAP, :], hT2[:, 0, f, :],
                                              slot[2][:, f * D + h * 512:f * D + (h + 1) * 512],
                                              start=(f == 0), stop=(f == 3))
                mm.then_inc(o["down"], 1)
                pe.wait_ge(o["ob"], 2 * k + 2)
                for t in range(TT):
                    for h in range(2):
                        i = 2 * t + h
                        if i >= 4:
                            pe.wait_ge(o["added"], 8 * k + i - 3)
                        nc.tensor.matmul(bank[i % 4][:, :], over_oT[:, t * P:(t + 1) * P], ob[0:CAP, h, :],
                                         start=True, stop=True).then_inc(o["sum"], 1)
            pe.sem_inc(o["down"], 1)
            further(pe, l, block_)

        at = 0
        qT, at = carve(AR, at, [HEADS // 2, T])
        KD, at = carve(AR, at, [KVH, T])
        Vt, at = carve(AR, at, [TT, KVH * HD])
        pT, at = carve(AR, at, [2, 8, P])
        dist, at = carve(AR, at, [2, SEQ])
        assert at <= 10764
        sqb = pT.rearrange("p a b c -> p (a b c)")[:, 0:2 * T].rearrange("p (a t) -> p a t", a=2)
        rsb = pT.rearrange("p a b c -> p (a b c)")[:, 2 * T:4 * T].rearrange("p (a t) -> p a t", a=2)
        xf = xn[:, :, :].rearrange("p a b -> p (a b)")
        Sb, _ = carve(xf, 0, [2, 4, SEQ])
        kraw, _ = carve(xf, 0, [2, T])
        ob_att, _ = carve(xf, 2048, [2, D])
        st = sb("st", [P, 2, 6, 4])
        NU = TT * KVH
        SCALE = HD ** -0.5
        SLOPE = [2.0 ** (-8.0 * (h + 1) / HEADS) for h in range(HEADS)]
        A_W = 104
        att_proj, att_raw, att_sq, att_ss, att_sqrt, att_n, att_kd, att_v = (
            sem(n) for n in ("att_proj", "att_raw", "att_sq", "att_ss", "att_sqrt", "att_n", "att_kd", "att_v"))
        s_done, s_ready, m_ready, p_ready, p_turned, pT_a, pT_d, o_done, o_ready, o_turned, oT_out = (
            sem(n) for n in ("s_done", "s_ready", "m_ready", "p_ready", "p_turned", "pT_a", "pT_d", "o_done",
                             "o_ready", "o_turned", "oT_out"))
        att_out_done = sem("att_out_done")

        def sp_att(sp):
            m = moe[0]
            for k in range(3):
                n = A_W + k
                sp.wait_ge(m["gu_done"] if k < 2 else m["down_done"], EXPERTS - 1)
                if k == 1:
                    sp.wait_ge(x_updated, 16)
                sp.dma_start(slot[n % SLOTS].rearrange("p (c f) -> p c f", c=KC),
                             a["att_w_in"][0, :, 512 * k:512 * (k + 1)].rearrange("(c p) f -> p c f", p=P)
                             ).then_inc(slot_loaded[n % SLOTS], 16)
            for k in range(2):
                n = A_W + 3 + k
                sp.wait_ge(m["gu_done"], EXPERTS)
                sp.dma_start(slot[n % SLOTS].rearrange("p (c f) -> p c f", c=KC),
                             a["att_w_out"][0, :, 512 * k:512 * (k + 1)].rearrange("(c p) f -> p c f", p=P)
                             ).then_inc(slot_loaded[n % SLOTS], 16)

        def pe_att(pe):
            pe_turn_norm(pe, 2)
            pe.wait_ge(hT_ready, KC * 3)

            def ss(i):
                pe.wait_ge(att_sq, i + 1)
                if i >= 2:
                    pe.wait_ge(att_sqrt, i - 1)
                nc.tensor.matmul(bank[6 + i % 2][:, :], blk[:, :], sqb[:, i % 2, :], start=True, stop=True).then_inc(att_ss, 1)
            for i in range(10):
                n = A_W + i // 4
                if i % 4 == 0:
                    pe.wait_ge(slot_loaded[n % SLOTS], 16 * (n // SLOTS + 1))
                if i >= 4:
                    pe.wait_ge(att_sq, i - 3)
                W = slot[n % SLOTS].rearrange("p (c f) -> p c f", c=KC)
                for c in range(KC):
                    mm = nc.tensor.matmul(bank[2 + i % 4][:, :], W[:, c, (i % 4) * P:(i % 4 + 1) * P], hT[:, c, :],
                                          start=(c == 0), stop=(c == KC - 1))
                mm.then_inc(att_proj, 1)
                if i:
                    ss(i - 1)
            W = slot[(A_W + 2) % SLOTS].rearrange("p (c f) -> p c f", c=KC)
            for t in range(TT):
                i = 10 + t
                pe.wait_ge(att_sq, min(i - 3, 10))
                for c in range(KC):
                    mm = nc.tensor.matmul(bank[2 + i % 4][:, 0:256], hT[:, c, t * P:(t + 1) * P], W[:, c, 256:512],
                                          start=(c == 0), stop=(c == KC - 1))
                mm.then_inc(att_proj, 1)
                if t == 0:
                    ss(9)
            pe.wait_ge(att_kd, 8)
            pe.wait_ge(att_n, 10)
            pe.wait_ge(att_v, TT)

            def scores(w):
                t, j = w // KVH, w % KVH
                if w >= 2:
                    pe.wait_ge(s_ready, 4 * (w - 1))
                for i in range(4):
                    h = 4 * j + i
                    hs = slice((h % 2) * HD, (h % 2) * HD + HD)
                    o = bank[2 * (w % 2) + h % 2][:, (i // 2) * SEQ:(i // 2 + 1) * SEQ]
                    mm = nc.tensor.matmul(o, qT[hs, h // 2, t * P:(t + 1) * P], KD[hs, j, (t // 2) * SEQ:(t // 2 + 1) * SEQ],
                                          start=True, stop=True)
                mm.then_inc(s_done, 1)
            scores(0)
            for w in range(NU + 2):
                if w + 1 < NU:
                    scores(w + 1)
                if w >= 2 and (w - 2) % KVH == KVH - 1:
                    pe.wait_ge(pT_a, min(w, NU))
                    pe.wait_ge(pT_d, min(w, NU))
                    pe.wait_ge(o_ready, w - 1)
                    t = (w - 2) // KVH
                    for c in range(KC):
                        mm = nc.tensor.transpose(bank[4 + c // 4][:, (c % 4) * P:(c % 4 + 1) * P],
                                                 ob_att[:, t % 2, c * P:(c + 1) * P], ident[:, :])
                    mm.then_inc(o_turned, 1)
                if w < NU:
                    pe.wait_ge(p_ready, w + 1)
                    if w:
                        pe.wait_ge(pT_a, w)
                        pe.wait_ge(pT_d, w)
                    if w >= 2 and (w - 2) % KVH == KVH - 1:
                        pe.wait_ge(oT_out, 2 * ((w - 2) // KVH + 1))
                    for i in range(4):
                        for kc in range(2):
                            mm = nc.tensor.transpose(bank[4 + i // 2][:, ((i % 2) * 2 + kc) * P:((i % 2) * 2 + kc + 1) * P],
                                                     Sb[:, w % 2, i, kc * P:(kc + 1) * P], ident[:, :])
                    mm.then_inc(p_turned, 1)
                if 1 <= w <= NU:
                    v = w - 1
                    t, j = v // KVH, v % KVH
                    pe.wait_ge(pT_a, v + 1)
                    pe.wait_ge(pT_d, v + 1)
                    if v >= 2:
                        pe.wait_ge(o_ready, v - 1)
                    for i in range(4):
                        for kc in range(2):
                            mm = nc.tensor.matmul(bank[6 + v % 2][:, i * HD:(i + 1) * HD], pT[:, v % 2, 2 * i + kc, :],
                                                  Vt[:, 2 * (t // 2) + kc, j * HD:(j + 1) * HD], start=(kc == 0),
                                                  stop=(kc == 1))
                    mm.then_inc(o_done, 1)
            pe.wait_ge(oT_out, 2 * TT)
            for h in range(2):
                n = A_W + 3 + h
                pe.wait_ge(slot_loaded[n % SLOTS], 16 * (n // SLOTS + 1))
                W = slot[n % SLOTS].rearrange("p (c f) -> p c f", c=KC)
                for t in range(TT):
                    i = h * TT + t
                    if i >= 4:
                        pe.wait_ge(x_updated, 16 + i - 3)
                    for c in range(KC):
                        mm = nc.tensor.matmul(bank[4 + i % 4][:, :], hT[:, c, t * P:(t + 1) * P], W[:, c, :],
                                              start=(c == 0), stop=(c == KC - 1))
                    mm.then_inc(att_out_done, 1)

        def act_att(act):
            for i in range(10):
                act.wait_ge(att_proj, i + 1)
                src = bank[2 + i % 4][:, :]
                nc.scalar.activation(qT[:, i, :] if i < 8 else kraw[:, i - 8, :], src, ACT.Copy).then_inc(att_raw, 1)
                if i >= 2:
                    act.wait_ge(att_ss, i - 1)
                nc.scalar.activation(sqb[:, i % 2, :], src, ACT.Square).then_inc(att_sq, 1)
                if i:
                    act_ss(act, i - 1)
            act_ss(act, 9)
            for t in range(TT):
                act.wait_ge(att_proj, 11 + t)
                nc.scalar.activation(Vt[:, t, :], bank[2 + (10 + t) % 4][:, 0:256], ACT.Copy).then_inc(att_v, 1)
            act.wait_ge(att_n, 10)
            for j in range(KVH):
                lo = (j % 2) * HD
                nc.scalar.activation(KD[0:HD, j, :], kraw[lo:lo + HD, j // 2, :], ACT.Copy).then_inc(att_kd, 1)
            for w in range(NU + 2):
                if w < NU:
                    act.wait_ge(m_ready, w + 1)
                    for i in range(4):
                        nc.scalar.activation(Sb[:, w % 2, i, :], Sb[:, w % 2, i, :], ACT.Exp, scale=SCALE,
                                             bias=st[:, w % 2, 1, i:i + 1], accum_out=st[:, w % 2, 2, i:i + 1])
                    nc.scalar.activation(st[:, w % 2, 3, :], st[:, w % 2, 4, :], ACT.Exp).then_inc(p_ready, 1)
                if 1 <= w <= NU:
                    v = w - 1
                    act.wait_ge(p_turned, v + 1)
                    if v >= 2:
                        act.wait_ge(o_done, v - 1)
                    nc.scalar.activation(pT[:, v % 2, 0:4, :].rearrange("p a b -> p (a b)"), bank[4][:, :],
                                         ACT.Copy).then_inc(pT_a, 1)
                if w >= 2 and (w - 2) % KVH == KVH - 1:
                    t = (w - 2) // KVH
                    act.wait_ge(o_turned, t + 1)
                    for c in range(2):
                        nc.scalar.activation(hT[:, 4 * c:4 * c + 4, t * P:(t + 1) * P],
                                             bank[4 + c][:, :].rearrange("p (c t) -> p c t", c=4), ACT.Copy).then_inc(oT_out, 1)

        def act_ss(act, i):
            act.wait_ge(att_ss, i + 1)
            if i >= 2:
                act.wait_ge(att_n, i - 1)
            nc.scalar.activation(rsb[:, i % 2, :], bank[6 + i % 2][:, :], ACT.Sqrt, scale=1.0 / HD,
                                 bias=eps_rms).then_inc(att_sqrt, 1)

        def dve_att(dve, step):
            dve_norm(dve, step, 2)
            for i in range(2):
                step(nc.vector.tensor_copy(dist[:, i, :], iota_i))
                step(nc.vector.tensor_scalar(dist[:, i, :], dist[:, i, :], -128.0 * i, None, ALU.add))
                step(nc.vector.tensor_scalar(dist[:, i, :], dist[:, i, :], pcol[:, 0:1], None, ALU.subtract))
                step(nc.vector.scalar_tensor_tensor(dist[:, i, :], dist[:, i, :], -1.0, dist[:, i, :], ALU.mult, ALU.max))
                far = Zb[:, 0:2, :].rearrange("p a b -> p (a b)")
                step(nc.vector.tensor_scalar(far, dist[:, i, :], float(P), 1e32, ALU.is_gt, ALU.mult))
                step(nc.vector.tensor_tensor(dist[:, i, :], dist[:, i, :], far, ALU.add))
            for i in range(10):
                dve.wait_ge(att_sqrt, i + 1)
                step(nc.vector.reciprocal(rsb[:, i % 2, :], rsb[:, i % 2, :]))
                x = qT[:, i, :] if i < 8 else kraw[:, i - 8, :]
                g = VB[:, B_QK + (i >= 8):B_QK + (i >= 8) + 1]
                nc.vector.scalar_tensor_tensor(x, x, g, rsb[:, i % 2, :], ALU.mult, ALU.mult).then_inc(att_n, 1)
            dve.wait_ge(att_n, 10)
            for j in range(KVH):
                lo = (j % 2) * HD
                nc.vector.tensor_copy(KD[HD:P, j, :], kraw[lo:lo + HD, j // 2, :]).then_inc(att_kd, 1)
            dve.wait_ge(att_kd, 8)
            for w in range(NU + 2):
                if w < NU:
                    t, j, par = w // KVH, w % KVH, w % 2
                    S_, s_ = Sb[:, par, :, :], st[:, par, :, :]
                    dve.wait_ge(s_done, w + 1)
                    if w >= 2:
                        dve.wait_ge(p_turned, w - 1)
                    for i in range(4):
                        h = 4 * j + i
                        nc.vector.scalar_tensor_tensor(S_[:, i, :], dist[:, t % 2, :], -SLOPE[h] / SCALE,
                                                       bank[2 * par + h % 2][:, (i // 2) * SEQ:(i // 2 + 1) * SEQ],
                                                       ALU.mult, ALU.add).then_inc(s_ready, 1)
                    dve.wait_ge(s_ready, 4 * (w + 1))
                    step(nc.vector.tensor_reduce(s_[:, 0, :], S_, AX.X, ALU.max))
                    sink = bb[:, 4 * j:4 * j + 4]
                    step(nc.vector.scalar_tensor_tensor(s_[:, 0, :], s_[:, 0, :], SCALE, sink, ALU.mult, ALU.max))
                    step(nc.vector.tensor_scalar(s_[:, 1, :], s_[:, 0, :], -1.0, None, ALU.mult))
                    nc.vector.tensor_tensor(s_[:, 4, :], sink, s_[:, 1, :], ALU.add).then_inc(m_ready, 1)
                if 1 <= w <= NU:
                    v = w - 1
                    par = v % 2
                    s_ = st[:, par, :, :]
                    dve.wait_ge(p_turned, v + 1)
                    nc.vector.tensor_copy(pT[:, par, 4:8, :].rearrange("p a b -> p (a b)"), bank[5][:, :]).then_inc(pT_d, 1)
                    if v >= 2:
                        dve.wait_ge(o_ready, v - 1)
                    step(nc.vector.tensor_tensor(s_[:, 5, :], s_[:, 2, :], s_[:, 3, :], ALU.add))
                    step(nc.vector.reciprocal(s_[:, 5, :], s_[:, 5, :]))
                if w >= 2:
                    v = w - 2
                    t, j, par = v // KVH, v % KVH, v % 2
                    s_ = st[:, par, :, :]
                    dve.wait_ge(o_done, v + 1)
                    if t >= 2 and j == 0:
                        dve.wait_ge(o_turned, t - 1)
                    nc.vector.tensor_tensor(ob_att[:, t % 2, j * 256:(j + 1) * 256].rearrange("p (h d) -> p h d", h=4),
                                            bank[6 + par][:, 0:256].rearrange("p (h d) -> p h d", h=4),
                                            s_[:, 5, :].unsqueeze(2).to_broadcast([P, 4, HD]), ALU.mult).then_inc(o_ready, 1)
            for h in range(2):
                for t in range(TT):
                    i = h * TT + t
                    dve.wait_ge(att_out_done, i + 1)
                    x = X[:, t, h * 512:(h + 1) * 512]
                    nc.vector.tensor_tensor(x, x, bank[4 + i % 4][:, :], ALU.add).then_inc(x_updated, 1)

        m0 = moe[0]
        FIRST = ([[(gn_out, FT)], [], [], [], [(out_done, 4)], [(out_done, 8)]],
                 [[(m0["down_done"], EXPERTS)], [(att_proj, 4)], [(att_proj, 8)], [(att_proj, 14)],
                  [(att_out_done, 4)], [(att_out_done, 8)]])

        pcol = sb("pcol", [P, 1])

        def pool_iota():
            ins = nc.gpsimd.iota(iota_i, pattern=[[1, SEQ]], base=0, channel_multiplier=0)
            ins.then_inc(iota_ready, 1)
            nc.gpsimd.iota(dest[:, 0:1].bitcast(mybir.dt.int32), pattern=[[0, 1]], base=0, channel_multiplier=1
                           ).then_inc(iota_ready, 1)

        def dve_tables(dve, step):
            dve.wait_ge(iota_ready, 2)
            step(nc.vector.tensor_copy(iota64[:, :], iota_i[:, 0:CAP]))
            step(nc.vector.tensor_copy(pcol[:, :], dest[:, 0:1].bitcast(mybir.dt.int32)))
            step(nc.vector.tensor_scalar(tie[:, :], iota64[:, 0:EPG], -1.0, float(EPG), ALU.mult, ALU.add))
            step(nc.vector.tensor_scalar(ebase[:, :], iota64[:, 0:EXPERTS], float(CAP), None, ALU.mult))
            dve.wait_ge(bb_raw, 1)
            step(nc.vector.tensor_copy(bb[:, :], bank[5][:, 0:HEADS + 72]))
            nc.vector.memset(small[:, 58:59], 0.0).then_inc(tables_ready, 1)

        def sp_rest(sp):
            sp_moe(sp, 0)
            sp_att(sp)
            sp_moe(sp, 1)
            for t in range(TT):
                sp.wait_ge(x_updated, 29 + t)
                y = (y_prompt, y_sample)[t // 2]
                sp.dma_start(y[0, (t % 2) * P:(t % 2 + 1) * P, :], X[:, t, :]).then_inc(y_stored, 16)
            sp.wait_ge(y_stored, 16 * TT)

        def pool_rest(pool):
            pool.wait_ge(gn_out, FT)
            pool_iota()
            pool_moe(pool, 0)
            pool_moe(pool, 1)

        def act_rest(act):
            act_norm(act, 1)
            act_hT(act, 1)
            act_moe(act, 0)
            act_norm(act, 2)
            act_hT(act, 2)
            act_att(act)
            act_norm(act, 3)
            act_hT(act, 3)
            act_moe(act, 1)

        def dve_rest(dve, step):
            dve_tables(dve, step)
            dve_moe(dve, step, 0)
            dve_att(dve, step)
            dve_moe(dve, step, 1)

        def pe_rest(pe):
            pe.wait_ge(brow_loaded, 80)
            pe.wait_ge(x_updated, 8)
            nc.tensor.matmul(bank[5][:, 0:HEADS + 72], ones[0:1, :], brow[0:1, :], start=True, stop=True).then_inc(bb_raw, 1)
            pe.wait_ge(tables_ready, 1)
            pe_moe(pe, 0)
            pe_att(pe)
            pe_moe(pe, 1)

        @block.sync
        def _(sp):
            for s, x in enumerate((a["x_prompt"], a["x_sample"])):
                sp.dma_start(X[:, 2 * s:2 * s + 2, :], x[0].rearrange("(t p) d -> p t d", p=P)).then_inc(x_loaded, 16)
            for n in range(6):
                if n == 1:
                    sp.wait_ge(vec_loaded, 16 * 20)
                w = min(512, REC_IN - 512 * n)
                sp.dma_start(slot[n][:, 0:KC * w].rearrange("p (c f) -> p c f", c=KC),
                             a["rec_w_in"][0, :, 512 * n:512 * n + w].rearrange("(c p) f -> p c f", p=P)
                             ).then_inc(slot_loaded[n], 16)
            sp.dma_start(brow[0:1, 0:HEADS], a["att_sink"]).then_inc(brow_loaded, 16)
            for l in range(2):
                b = HEADS + 36 * l
                sp.dma_start(brow[0:1, b:b + 4], a["moe_bg1"][l:l + 1, :]).then_inc(brow_loaded, 16)
                sp.dma_start(brow[0:1, b + 4:b + 36], a["moe_bg2"][l:l + 1].rearrange("a g e -> a (g e)")
                              ).then_inc(brow_loaded, 16)
            sp.wait_ge(rgw_zero, 2)
            for W, name in ((WA, "rg_wa"), (WX, "rg_wx")):
                for h in range(2):
                    for d in range(2):
                        sp.dma_start(W[h * HD:h * HD + HD, d * FT:d * FT + FT, h * HD:h * HD + HD],
                                      a[name][0, d].rearrange("(f h) c e -> h c f e", h=2)[h]).then_inc(rgw_loaded, 16)
            sp.dma_start(LUP[0:32, :, :], a["rw_w_up"][0].rearrange("d r f -> r d f")).then_inc(rgw_loaded, 16)
            sp.dma_start(LUP[32:64, :, :], a["rw_a_up"][0].rearrange("d r f -> r d f")).then_inc(rgw_loaded, 16)
            sp.dma_start(LUP[64:128, 0, :], a["rw_g_up"][0]).then_inc(rgw_loaded, 16)
            for l in range(2):
                sp.dma_start(wr[:, l, :, 0:4], a["moe_wg1"][l].rearrange("(c p) g -> p c g", p=P)).then_inc(router_loaded, 16)
                for g in range(GROUPS):
                    sp.dma_start(wr[:, l, :, 4 + g * EPG:4 + g * EPG + EPG],
                                  a["moe_wg2"][l, g].rearrange("(c p) e -> p c e", p=P)).then_inc(router_loaded, 16)
            for n in (6, 7):
                if n == 6:
                    sp.wait_ge(ys_done, 16)
                sp.dma_start(slot[n - 6].rearrange("p (c f) -> p c f", c=KC),
                             a["rec_w_out"][0, :, 512 * (n - 6):512 * (n - 5)].rearrange("(c p) f -> p c f", p=P)
                             ).then_inc(slot_loaded[n - 6], 16)
            sp_rest(sp)

        @block.gpsimd
        def _(pool):
            n = [0]

            def step(ins):
                n[0] += 1
                ins.then_inc(pool_step, 1)
                pool.wait_ge(pool_step, n[0])
            nc.gpsimd.memset(ident[:, :], 0.0)
            nc.gpsimd.memset(eps_rms, RMS_EPS)
            nc.gpsimd.memset(eps_gn, RW_EPS)
            step(nc.gpsimd.memset(ones[:, :], 1.0))
            nc.gpsimd.affine_select(out=ident[:, :], in_=ident[:, :], compare_op=ALU.not_equal, fill=1.0, base=0,
                                    pattern=[[-1, P]], channel_multiplier=1).then_inc(ident_ready, 1)
            nc.gpsimd.memset(WA, 0.0).then_inc(rgw_zero, 1)
            nc.gpsimd.memset(WX, 0.0).then_inc(rgw_zero, 1)
            nc.gpsimd.memset(lvlmask[:, :, :, :], 0.0)
            step(nc.gpsimd.memset(blk[:, :], 0.0))
            step(nc.gpsimd.memset(blk[0:HD, 0:HD], 1.0))
            step(nc.gpsimd.memset(blk[HD:P, HD:P], 1.0))
            for d in range(2):
                sgn = 1 - 2 * d
                for k in range(4):
                    ins = nc.gpsimd.affine_select(out=chunkmask[:, d, k, :], in_=ones[:, :],
                                                  compare_op=ALU.is_ge if k % 2 else ALU.is_gt,
                                                  fill=0.0, base=0, pattern=[[sgn, P]], channel_multiplier=-sgn)
                for l in range(LEVELS):
                    B = 2 ** l
                    nq = P // (2 * B)
                    v = lvlmask[:, d, l, :].rearrange("p (q h r) -> p q h r", q=nq, h=2)[:, :, d, :]
                    low, high = (B, 2 * B - 1) if d == 0 else (0, B - 1)
                    step(nc.gpsimd.affine_select(out=v, in_=ones[:, :].rearrange("p (q h r) -> p q h r", q=nq, h=2)[:, :, d, :],
                                                 compare_op=ALU.is_ge, fill=0.0, base=-low,
                                                 pattern=[[-2 * B, nq], [0, B]], channel_multiplier=1))
                    step(nc.gpsimd.affine_select(out=v, in_=v, compare_op=ALU.is_ge, fill=0.0, base=high,
                                                 pattern=[[2 * B, nq], [0, B]], channel_multiplier=-1))
            nc.gpsimd.memset(small[:, 56:57], 0.0).then_inc(consts_ready, 1)
            pool.wait_ge(gemm_out, 8)
            for ft in range(FT):
                g = ksq[:, ft, :]
                step(nc.gpsimd.tensor_tensor(g, rgg[:, ft, :], rgg[:, ft, :], ALU.mult))
                step(nc.gpsimd.tensor_scalar(g, g, 0.044715, 1.0, ALU.mult, ALU.add))
                nc.gpsimd.tensor_tensor(g, g, rgg[:, ft, :], ALU.mult).then_inc(gelu_in, 1)
                pool.wait_ge(gelu_tanh, ft + 1)
                step(nc.gpsimd.tensor_scalar(g, g, 0.5, 0.5, ALU.mult, ALU.add))
                nc.gpsimd.tensor_tensor(rgg[:, ft, :], rgg[:, ft, :], g, ALU.mult).then_inc(gelu_ready, 1)
            def copy_values(ft):
                nc.gpsimd.tensor_copy(vcur, vT[:, bass.ds(ft, 1), :].rearrange("p a b -> p (a b)")).then_inc(vcur_ready, 1)

            def add_outputs(ft):
                for s in range(2):
                    pool.wait_ge(ys_out, 3 * (2 * ft + 1) + 3 + s)
                    dst = y_chunks(ft, 1 - s)
                    nc.gpsimd.tensor_tensor(dst, dst, yback[:, s, :].rearrange("p (b t) -> p b t", b=NSEQ),
                                            ALU.add).then_inc(y_added, 1)
            pool.wait_ge(gemm_done, G_UNIT)
            nc.gpsimd.memset(Sst, 0.0).then_inc(sst_zero, 1)
            pool.wait_ge(pad_free, 17)
            nc.gpsimd.memset(small[:, 58:59], 0.0).then_inc(y_added, 1)
            copy_values(0)
            with pool.Fori(0, FT - 1) as ft:
                pool.wait_ge(v_turned, ft + 1)
                copy_values(ft + 1)
                add_outputs(ft)
            add_outputs(FT - 1)
            pool_rest(pool)


        @block.scalar
        def _(act):
            for name, r in (("norm_mix", V_MIX), ("norm_ffn", V_FFN), ("rg_conv_w", V_CW), ("rg_conv_b", V_CB),
                            ("rg_ba", V_BA), ("rg_bx", V_BX), ("rg_lambda", V_LAM), ("rw_w0", V_W0), ("rw_a0", V_A0),
                            ("rw_k_k", V_KK), ("rw_k_a", V_KA), ("rw_r_k", V_RK), ("rw_ln_w", V_LNW),
                            ("rw_ln_b", V_LNB)):
                v = row(name)
                act.dma_start(vrows[r:r + v.shape[0], 0, :], v).then_inc(vec_loaded, 16)
            for name, r in (("rw_mu_l", B_MUL), ("rw_mu_r", B_MUR)):
                v = row(name)
                act.dma_start(vrows[r:r + v.shape[0], 1, :], v).then_inc(vec_loaded, 16)
            for k, name in enumerate(("att_q_norm", "att_k_norm")):
                for h in range(2):
                    act.dma_start(vrows[B_QK + k:B_QK + k + 1, 1, h * HD:h * HD + HD], a[name]).then_inc(vec_loaded, 16)
            act.wait_ge(ident_ready, 1)
            act_norm(act, 0)
            act_hT(act, 0)

            n = [0]

            def step(ins):
                n[0] += 1
                ins.then_inc(act_step, 1)
                act.wait_ge(act_step, n[0])

            act.wait_ge(v_ready, 2)
            step(nc.scalar.activation(lt[:, 0:8], VA[:, V_LAM:V_LAM + 8], ACT.Abs))
            step(nc.scalar.activation(lt[:, 0:8], lt[:, 0:8], ACT.Exp, scale=-1.0))
            nc.scalar.activation(lt[:, 8:16], lt[:, 0:8], ACT.Ln, bias=one_col).then_inc(lam_ready, 1)

            j = 0
            for f in range(NF):
                act.wait_ge(gemm_done, f + 1)
                src = bank[2 + f % 4][:, :]
                if 4 <= f < 8:
                    nc.scalar.activation(rgg[:, f - 4, :], src, ACT.Copy).then_inc(gemm_out, 1)
                    continue
                if j == 0:
                    act.wait_ge(pad_zero, 1)
                if j >= 2:
                    act.wait_ge(pad_free, j - 1)
                nc.scalar.activation(pad[:, j % 2, :, 2:2 + SEQ], src.rearrange("p (s t) -> p s t", s=NSEQ),
                                     ACT.Copy).then_inc(gemm_out, 1)
                j += 1
                if f in (10, 12, 14, 16):
                    ft = (f - 10) // 2
                    act.wait_ge(gelu_in, ft + 1)
                    nc.scalar.activation(ksq[:, ft, :], ksq[:, ft, :], ACT.Tanh,
                                         scale=float(np.sqrt(2 / np.pi))).then_inc(gelu_tanh, 1)
                if f == NF - 2:
                    act.wait_ge(gelu_ready, FT)
                    for ft in range(FT):
                        act.wait_ge(kk_raw, ft + 1)
                        nc.scalar.activation(ksq[:, ft, :], kk[:, ft, :], ACT.Square).then_inc(kk_sq, 1)
            for ft in range(FT):
                act.wait_ge(gemm_done, G_KK + ft + 1)
                nc.scalar.activation(kinv[:, ft, :], bank[2 + (G_KK + ft) % 4][:, :], ACT.Sqrt).then_inc(gemm_out, 1)
            act.wait_ge(mixed_in, NF - 8)
            nc.scalar.activation(wag[64:128], wag[64:128], ACT.Sigmoid).then_inc(wag_act, 1)
            nc.scalar.activation(wag[0:32], wag[0:32], ACT.Tanh).then_inc(wag_act, 1)
            g = G_RG
            for ft in range(FT):
                for d in range(2):
                    for w, b in enumerate((V_BA, V_BX)):
                        act.wait_ge(gemm_done, g + 1)
                        c = b + d * FT + ft
                        nc.scalar.activation(gates[:, d, ft, w * T:(w + 1) * T], bank[2 + g % 4][:, :], ACT.Sigmoid,
                                             bias=VA[:, c:c + 1]).then_inc(gemm_out, 1)
                        g += 1
            for u in range(8):
                ft, d = u // 2, u % 2
                act.wait_ge(gemm_done, g + 1)
                if u >= 2:
                    act.wait_ge(sg_free, u - 1)
                c = V_W0 + d * FT + ft
                nc.scalar.activation(tmpA[:, u % 2, :], bank[2 + g % 4][:, :], ACT.Sigmoid,
                                     bias=VA[:, c:c + 1]).then_inc(gemm_out, 1)
                act.wait_ge(gemm_done, g + 2)
                c = V_A0 + d * FT + ft
                nc.scalar.activation(asg[:, u, :], bank[2 + (g + 1) % 4][:, :], ACT.Sigmoid,
                                     bias=VA[:, c:c + 1]).then_inc(gemm_out, 1)
                g += 2
            act.wait_ge(sp_ready, 1)
            for d in range(2):
                for ft in range(FT):
                    c = d * FT + ft
                    r = gates[:, d, ft, 0:T]
                    if d == 0:
                        act.wait_ge(sg_free, 8)
                    else:
                        act.wait_ge(rg_done, ft + 1)
                    step(nc.scalar.activation(q4[:, ft, :], r, ACT.Tanh, scale=sp8[:, c:c + 1]))
                    nc.scalar.activation(r, r, ACT.Exp, scale=nsp8[:, c:c + 1]).then_inc(rg_exp, 1)
                for ft in range(FT):
                    act.wait_ge(rg_q, d * FT + ft + 1)
                    nc.scalar.activation(q4[:, ft, :], q4[:, ft, :], ACT.Sqrt).then_inc(rg_sqrt, 1)
            e2 = E2.rearrange("p a b c -> p (a b c)")
            def exp_factors(ft, d):
                act.wait_ge(prep_ready, 2 * ft + d + 1)
                for k in range(2):
                    ins = nc.scalar.activation(
                        E2[:, k, :, :].rearrange("p a b -> p (a b)"),
                        P0[:, bass.ds(2 * ft + d, 1), :, :].rearrange("p u a b -> p (u a b)"),
                        ACT.Exp, scale=(1 if k else -1) * DECAY)
                ins.then_inc(exp_ready, 1)

            def turned_copies(ft, d):
                if d == 0:
                    act.wait_ge(v_turned, ft + 1)
                    nc.scalar.activation(Vtok, bank[6][:, :], ACT.Copy)
                act.wait_ge(bk_turned, 2 * ft + d + 1)
                nc.scalar.activation(BKtok, bank[7][:, :], ACT.Copy).then_inc(bktok_ready, 1)

            def rhs_copy(ft, d, s):
                act.wait_ge(rhs_done, 2 * (2 * ft + d) + s + 1)
                nc.scalar.activation(RU[:, 0, :], bank[6][:, 0:256], ACT.Copy).then_inc(rhs_out, 1)

            def u_copy(ft, d, s):
                act.wait_ge(u_done, 2 * (2 * ft + d) + s + 1)
                nc.scalar.activation(RU[:, 1, :], bank[6][:, 256:512], ACT.Copy).then_inc(u_out, 1)

            def output_copies(ft, d, s):
                act.wait_ge(ys_done, 2 * (2 * ft + d) + s + 1)
                if s == 0:
                    for b in range(NSEQ):
                        for h in range(2):
                            hs = slice(h * HD, h * HD + HD)
                            ins = nc.scalar.activation(Sst[hs, b, hs], bank[7][hs, 256 + b * HD:256 + (b + 1) * HD],
                                                       ACT.Copy, scale=sscale[hs, d, b:b + 1])
                    ins.then_inc(ys_out, 1)
                src = bank[7][:, 0:256]
                if d == 0:
                    ins = nc.scalar.activation(y_chunks(ft, s), src.rearrange("p (b t) -> p b t", b=NSEQ), ACT.Copy)
                else:
                    act.wait_ge(y_added, 2 * ft + 1)
                    ins = nc.scalar.activation(yback[:, s, :], src, ACT.Copy)
                ins.then_inc(ys_out, 1)

            def unit_copies(ft, d, last, nxt):
                if last is not None:
                    turned_copies(*last)
                    rhs_copy(*last, 0)
                    u_copy(*last, 0)
                    output_copies(*last, 0)
                    rhs_copy(*last, 1)
                for l in range(1, LEVELS - 1):
                    if last is not None and l == 2:
                        output_copies(*last, 1)
                    for q in range(2):
                        act.wait_ge(t_turned, 10 * (2 * ft + d) + 2 * (l - 1) + q + 1)
                        nc.scalar.activation(Tb[d][:, 4 * q:4 * q + 4, 0, :],
                                             bank[4 + q][:, :].rearrange("p (k t) -> p k t", k=4),
                                             ACT.Copy).then_inc(t_copied, 1)
                    if last is not None and l == 1:
                        u_copy(*last, 1)
                    if nxt is not None and l == 2:
                        exp_factors(*nxt)
            act.wait_ge(sg_free, 8)
            exp_factors(0, 0)
            unit_copies(0, 0, None, (0, 1))
            with act.Fori(0, FT - 1) as ft:
                unit_copies(ft, 1, (ft, 0), (ft + 1, 0))
                unit_copies(ft + 1, 0, (ft, 1), (ft + 1, 1))
            unit_copies(FT - 1, 1, (FT - 1, 0), None)
            turned_copies(FT - 1, 1)
            for s in range(2):
                rhs_copy(FT - 1, 1, s)
                u_copy(FT - 1, 1, s)
                output_copies(FT - 1, 1, s)
            for ft in range(FT):
                act.wait_ge(gn_c, ft + 1)
                nc.scalar.activation(e2[:, 0:T], yT[:, ft, :], ACT.Square).then_inc(gn_sq, 1)
                act.wait_ge(gn_var, ft + 1)
                nc.scalar.activation(e2[:, T:2 * T], bank[1][:, :], ACT.Sqrt, scale=1.0 / HD,
                                     bias=eps_gn).then_inc(gn_sqrt, 1)
            act_rest(act)


        @block.vector
        def _(dve):
            n = [0]

            def step(ins):
                n[0] += 1
                ins.then_inc(dve_step, 1)
                dve.wait_ge(dve_step, n[0])
            nc.vector.memset(pad, 0.0).then_inc(pad_zero, 1)
            dve.wait_ge(vrows_turned, 1)
            nc.vector.tensor_copy(VA[:, :], bank[6][:, 0:V_END]).then_inc(v_ready, 1)
            nc.vector.tensor_copy(VB[:, :], bank[7][:, 0:B_END]).then_inc(v_ready, 1)
            dve.wait_ge(v_ready, 2)
            dve_norm(dve, step, 0)
            step(nc.vector.tensor_tensor(c0, VB[:, B_MUL:B_MUL + 13], VB[:, B_MUR:B_MUR + 13], ALU.add))
            step(nc.vector.tensor_scalar(c0, c0, -1.0, 1.0, ALU.mult, ALU.add))
            nc.vector.tensor_scalar(one_ka[:, :], VA[:, V_KA:V_KA + FT], -1.0, 1.0, ALU.mult, ALU.add)
            dve.wait_ge(lam_ready, 1)
            x, ln, u = lt[:, 0:8], lt[:, 8:16], lt[:, 16:24]
            step(nc.vector.tensor_scalar(u, x, 1.0, None, ALU.add))
            step(nc.vector.tensor_scalar(u, u, -1.0, 1e-30, ALU.add, ALU.add))
            step(nc.vector.reciprocal(u, u))
            step(nc.vector.scalar_tensor_tensor(ln, ln, 1e-30, u, ALU.add, ALU.mult))
            step(nc.vector.tensor_tensor(ln, ln, x, ALU.mult))
            step(nc.vector.tensor_scalar(u, VA[:, V_LAM:V_LAM + 8], -1.0, 0.0, ALU.mult, ALU.max))
            step(nc.vector.tensor_tensor(ln, ln, u, ALU.add))
            nc.vector.tensor_scalar(sp8, ln, 8.0, None, ALU.mult).then_inc(sp_ready, 0 + 1)
            nc.vector.tensor_scalar(nsp8, ln, -8.0, None, ALU.mult).then_inc(sp_ready, 1)

            j = 0
            for f in range(NF):
                if 4 <= f < 8:
                    continue
                dve.wait_ge(gemm_out, f + 1)
                row_ = pad[:, j % 2, :, :]
                if f < 4:
                    y = xc[:, f, :].rearrange("p (s t) -> p s t", s=NSEQ)
                    step(nc.vector.tensor_scalar(y, row_[:, :, 0:SEQ], VA[:, V_CW + f:V_CW + f + 1],
                                                 VA[:, V_CB + f:V_CB + f + 1], ALU.mult, ALU.add))
                    for k in range(1, CONV):
                        c = V_CW + k * FT + f
                        ins = nc.vector.scalar_tensor_tensor(y, row_[:, :, k:k + SEQ], VA[:, c:c + 1], y,
                                                             ALU.mult, ALU.add)
                        if k < CONV - 1:
                            step(ins)
                    ins.then_inc(pad_free, 1)
                else:
                    m = f - 8
                    y = (wag if m == 12 else (rT, kT, vT)[m // 4][:, m % 4, :]).rearrange("p (s t) -> p s t", s=NSEQ)
                    step(nc.vector.tensor_scalar(y, row_[:, :, 2:2 + SEQ], c0[:, m:m + 1], None, ALU.mult))
                    step(nc.vector.scalar_tensor_tensor(y, row_[:, :, 1:1 + SEQ], VB[:, B_MUL + m:B_MUL + m + 1], y,
                                                        ALU.mult, ALU.add))
                    nc.vector.scalar_tensor_tensor(y, row_[:, :, 3:3 + SEQ], VB[:, B_MUR + m:B_MUR + m + 1], y,
                                                   ALU.mult, ALU.add).then_inc(pad_free, 1)
                    dve.wait_ge(pad_free, j + 1)
                    if m == 7:
                        for ft in range(FT):
                            nc.vector.tensor_scalar(kk[:, ft, :], kT[:, ft, :], VA[:, V_KK + ft:V_KK + ft + 1], None,
                                                    ALU.mult).then_inc(kk_raw, 1)
                    if m == 12:
                        step(nc.vector.tensor_copy(small[:, 62:63], wag[:, T - 1:T]))
                        nc.vector.memset(small[:, 63:64], 0.0).then_inc(mixed_in, NF - 8)
                j += 1
            dve.wait_ge(gemm_out, G_KK + FT)
            step(nc.vector.tensor_scalar(kinv, kinv, 1e-12, None, ALU.max))
            step(nc.vector.reciprocal(kinv, kinv))
            dve.wait_ge(kk_raw, FT)
            nc.vector.tensor_tensor(kk, kk, kinv, ALU.mult).then_inc(kk_ready, 1)
            dve.wait_ge(consts_ready, 1)
            dve.wait_ge(gemm_out, G_RG)
            step(nc.vector.memset(P0[:, :, :, 0:1], 0.0))
            for u in range(8):
                dve.wait_ge(gemm_out, G_UNIT + 2 * u + 1)
                for c in range(TT):
                    ins = nc.vector.tensor_tensor_scan(P0[:, u, c, 1:P + 1], ones[:, :], tmpA[:, u % 2, c * P:(c + 1) * P],
                                                       0.0, ALU.mult, ALU.add)
                ins.then_inc(sg_free, 1)
                dve.wait_ge(sg_free, u + 1)
                step(nc.vector.tensor_copy(pm[:, u, :], P0[:, u, :, P // 2]))
                step(nc.vector.tensor_tensor(P0[:, u, :, :], P0[:, u, :, :],
                                             pm[:, u, :].unsqueeze(2).to_broadcast([P, TT, P + 1]), ALU.subtract))
            for d in range(2):
                for ft in range(FT):
                    dve.wait_ge(rg_exp, d * FT + ft + 1)
                    q, t1, aa = q4[:, ft, :], tmpB, gates[:, d, ft, 0:T]
                    step(nc.vector.tensor_tensor(t1, aa, aa, ALU.mult))
                    nc.vector.scalar_tensor_tensor(q, t1, 1.0, q, ALU.add, ALU.mult).then_inc(rg_q, 1)
                    dve.wait_ge(rg_q, d * FT + ft + 1)
                for ft in range(FT):
                    q, aa, ii = q4[:, ft, :], gates[:, d, ft, 0:T], gates[:, d, ft, T:2 * T]
                    step(nc.vector.tensor_tensor(ii, ii, xc[:, ft, :], ALU.mult))
                    dve.wait_ge(rg_sqrt, d * FT + ft + 1)
                    step(nc.vector.tensor_tensor(q, q, ii, ALU.mult))
                    for s in range(NSEQ):
                        if d == 0:
                            v = slice(s * SEQ, s * SEQ + SEQ)
                            ins = nc.vector.tensor_tensor_scan(ii[:, v], aa[:, v], q[:, v], 0.0, ALU.mult, ALU.add)
                        else:
                            ins = nc.vector.tensor_tensor_scan(
                                ii[:, s * SEQ:(s + 1) * SEQ][:, ::-1], aa[:, s * SEQ:(s + 1) * SEQ][:, ::-1],
                                q[:, s * SEQ:(s + 1) * SEQ][:, ::-1], 0.0, ALU.mult, ALU.add)
                    ins.then_inc(rg_done, 1)
            for ft in range(FT):
                h0, h1 = gates[:, 0, ft, T:2 * T], gates[:, 1, ft, T:2 * T]
                dve.wait_ge(rg_done, 2 * FT)
                step(nc.vector.tensor_tensor(h0, h0, h1, ALU.add))
                dve.wait_ge(gelu_ready, ft + 1)
                step(nc.vector.tensor_tensor(mixT[:, ft, :], h0, rgg[:, ft, :], ALU.mult))
            e2 = E2.rearrange("p a b c -> p (a b c)")
            dve.wait_ge(kk_ready, 1)

            nc.vector.memset(small[:, 59:60], 0.0).then_inc(prep_ready, 1)
            m3 = lambda v: v.rearrange("p (c t) -> p c t", c=TT)
            EP, EN = E2[:, 0, :, :], E2[:, 1, :, :]

            def unit_views(ft, d):
                tile = lambda t, k=None: m3(t[:, bass.ds(ft if k is None else k, 1), :].rearrange("p a b -> p (a b)"))
                col = lambda t, c: t[:, bass.ds(ft + c, 1)]
                return tile, col, BKt[d][:, 0, :, :], BKt[d][:, 1, :, :], ARt[d][:, :, 0, :], ARt[d][:, :, 1, :]

            def prepare(part, ft, d):
                tile, col, Bt, Kt, At, Rt = unit_views(ft, d)
                rate = tile(asg, 2 * ft + d)
                n = LOOP_STEPS * ft + 4 * d
                incl, excl, inv = ((EP[:, :, 1:], EP[:, :, :P], EN[:, :, 1:]) if d == 0 else
                                   (EN[:, :, :P], EN[:, :, 1:], EP[:, :, :P]))
                if part == 0:
                    nc.vector.tensor_scalar(Kt, rate, col(VA, V_KA), col(one_ka, 0), ALU.mult,
                                            ALU.add).then_inc(loop_step, 1)
                    dve.wait_ge(loop_step, n + 1)
                if part == 1:
                    nc.vector.tensor_tensor(Kt, Kt, tile(kT), ALU.mult).then_inc(loop_step, 1)
                    dve.wait_ge(loop_step, n + 2)
                    if d == 0:
                        nc.vector.tensor_copy(m3(ksum), Kt).then_inc(loop_step, 1)
                    else:
                        nc.vector.tensor_tensor(m3(ksum), m3(ksum), Kt, ALU.add).then_inc(loop_step, 1)
                    dve.wait_ge(loop_step, n + 3)
                if part == 2:
                    nc.vector.tensor_tensor(Bt, rate, tile(kk), ALU.mult).then_inc(loop_step, 1)
                    dve.wait_ge(loop_step, n + 4)
                if part == 3:
                    dve.wait_ge(exp_ready, 2 * ft + d + 1)
                    nc.vector.tensor_tensor(Kt, Kt, inv, ALU.mult)
                    nc.vector.tensor_tensor(Bt, Bt, inv, ALU.mult)
                if part == 4:
                    nc.vector.scalar_tensor_tensor(At, tile(kk), -1.0, excl, ALU.mult, ALU.mult)
                if part == 5:
                    nc.vector.tensor_tensor(Rt, tile(rT), incl, ALU.mult)
                    for b in range(NSEQ):
                        c1, c2 = (2 * b, 2 * b + 1) if d == 0 else (2 * b + 1, 2 * b)
                        e1, e2_ = (EP[:, c1, P:P + 1], EN[:, c2, 0:1]) if d == 0 else (EN[:, c1, 0:1], EP[:, c2, P:P + 1])
                        ins = nc.vector.tensor_tensor(sscale[:, d, b:b + 1], e1, e2_, ALU.mult)
                    ins.then_inc(prep_ready, 1)
                    if d == 1:
                        nc.vector.scalar_tensor_tensor(tile(kT), tile(rT), col(VA, V_RK), m3(ksum), ALU.mult,
                                                       ALU.mult).then_inc(loop_step, 1)
                        dve.wait_ge(loop_step, LOOP_STEPS * ft + 9)

            def masks_and_inverse(ft, d, nxt):
                u = 2 * ft + d
                M, Tt = Mb[d], Tb[d]
                m4 = lambda v: v.rearrange("p (k t) -> p k t", k=4)
                four = lambda v: v.unsqueeze(1).to_broadcast([P, 4, P])
                for p in range(8):
                    dve.wait_ge(m_done, 8 * u + p + 1)
                    nc.vector.tensor_tensor(M[:, p, :, :], m4(bank[p % 6][:, :]), chunkmask[:, d, :, :],
                                            ALU.mult).then_inc(m_out, 1)
                for l in range(LEVELS):
                    if l == 0:
                        dve.wait_ge(m_out, 8 * u + 8)
                        nc.vector.tensor_tensor(Tt[:, :, 1, :], M[:, :, 0, :],
                                                lvlmask[:, 1 - d, 0, :].unsqueeze(1).to_broadcast([P, 8, P]),
                                                ALU.mult).then_inc(t_block, 1)
                    for q in range(2):
                        dve.wait_ge(z_done, 14 * u + 2 * l + q + 1)
                        nc.vector.tensor_tensor(Zb[:, 4 * q:4 * q + 4, :], m4(bank[q][:, :]), four(lvlmask[:, d, l, :]),
                                                ALU.mult).then_inc(z_out, 1)
                    if nxt is not None and l in (3, 4, 5):
                        if l == 3:
                            dve.wait_ge(ys_out, 3 * u + 1)
                        prepare(2 * (l - 3), *nxt)
                    for q in range(2):
                        k = 12 * u + 2 * (l - 1) + q + 1
                        if l == 0:
                            dve.wait_ge(t_block, u + 1)
                            nc.vector.tensor_tensor(Tt[:, 4 * q:4 * q + 4, 1, :], Tt[:, 4 * q:4 * q + 4, 1, :],
                                                    four(ident[:, :]), ALU.add)
                            dve.wait_ge(z_out, 14 * u + q + 1)
                            ins = nc.vector.tensor_tensor(Tt[:, 4 * q:4 * q + 4, 0, :], Zb[:, 4 * q:4 * q + 4, :],
                                                          four(ident[:, :]), ALU.add)
                        else:
                            dve.wait_ge(t_done, k)
                            dst = Tt[:, 4 * q:4 * q + 4, 1, :]
                            ins = nc.vector.tensor_tensor(dst, m4(bank[2 + q][:, :]), dst, ALU.add)
                        ins.then_inc(t_out, 1)
                    if nxt is not None and l in (3, 4, 5):
                        prepare(2 * (l - 3) + 1, *nxt)
            for part in range(6):
                prepare(part, 0, 0)
            masks_and_inverse(0, 0, (0, 1))
            with dve.Fori(0, FT - 1) as ft:
                masks_and_inverse(ft, 1, (ft + 1, 0))
                masks_and_inverse(ft + 1, 0, (ft + 1, 1))
            masks_and_inverse(FT - 1, 1, None)

            dve.wait_ge(loop_step, FT * LOOP_STEPS)
            for ft in range(FT):
                y = yT[:, ft, :]
                dve.wait_ge(gn_mean, ft + 1)
                nc.vector.scalar_tensor_tensor(y, bank[0][:, :], -1.0 / HD, y, ALU.mult, ALU.add).then_inc(gn_c, 1)
                dve.wait_ge(gn_mm, ft + 1)
                t1, t2 = ARt[0].rearrange("p a b c -> p (a b c)")[:, 0:T], ARt[0].rearrange("p a b c -> p (a b c)")[:, T:2 * T]
                step(nc.vector.tensor_tensor(t1, bank[2][:, :], vT[:, ft, :], ALU.mult))
                dve.wait_ge(gn_sqrt, ft + 1)
                step(nc.vector.reciprocal(t2, e2[:, T:2 * T]))
                step(nc.vector.tensor_tensor(y, y, t2, ALU.mult))
                step(nc.vector.tensor_scalar(y, y, VA[:, V_LNW + ft:V_LNW + ft + 1], VA[:, V_LNB + ft:V_LNB + ft + 1],
                                             ALU.mult, ALU.add))
                step(nc.vector.tensor_tensor(y, y, t1, ALU.add))
                nc.vector.tensor_tensor(y, y, bank[3][:, :], ALU.mult).then_inc(gn_out, 1)
                dve.wait_ge(gn_out, ft + 1)
            for h in range(2):
                for t in range(TT):
                    i = h * TT + t
                    dve.wait_ge(out_done, i + 1)
                    x = X[:, t, h * 512:(h + 1) * 512]
                    nc.vector.tensor_tensor(x, x, bank[4 + i % 4][:, :], ALU.add).then_inc(x_updated, 1)
            dve_rest(dve, step)


        @block.tensor
        def _(pe):
            pe.wait_ge(ident_ready, 1)
            pe.wait_ge(vec_loaded, 16 * 20)
            nc.tensor.transpose(bank[6][:, 0:V_END], vrows[0:V_END, 0, :], ident[0:V_END, 0:V_END])
            nc.tensor.transpose(bank[7][:, 0:B_END], vrows[0:B_END, 1, :], ident[0:B_END, 0:B_END]).then_inc(vrows_turned, 1)
            pe_turn_norm(pe, 0)

            def out_bank(g):
                if g >= 4:
                    pe.wait_ge(gemm_out, g - 3)
                return bank[2 + g % 4][:, :]
            pe.wait_ge(hT_ready, KC)
            for f in range(NF):
                n = f // 4
                w = min(512, REC_IN - 512 * n)
                W = slot[n][:, 0:KC * w].rearrange("p (c f) -> p c f", c=KC)
                if f % 4 == 0:
                    pe.wait_ge(slot_loaded[n], 16)
                o = out_bank(f)
                for c in range(KC):
                    mm = nc.tensor.matmul(o, W[:, c, (f % 4) * P:(f % 4 + 1) * P], hT[:, c, :], start=(c == 0), stop=(c == KC - 1))
                mm.then_inc(gemm_done, 1)
            g = G_KK
            pe.wait_ge(consts_ready, 1)
            for ft in range(FT):
                pe.wait_ge(kk_sq, ft + 1)
                nc.tensor.matmul(out_bank(g), blk[:, :], ksq[:, ft, :], start=True, stop=True).then_inc(gemm_done, 1)
                g += 1
            pe.wait_ge(rgw_loaded, 16 * 11)
            pe.wait_ge(pad_free, FT)
            for ft in range(FT):
                for d in range(2):
                    for W in (WA, WX):
                        nc.tensor.matmul(out_bank(g), W[:, d * FT + ft, :], xc[:, ft, :], start=True, stop=True).then_inc(gemm_done, 1)
                        g += 1
            pe.wait_ge(wag_act, 2)
            for u in range(8):
                ft, d = u // 2, u % 2
                for lo in (0, 32):
                    nc.tensor.matmul(out_bank(g), LUP[lo:lo + 32, d, ft * P:(ft + 1) * P], wag[lo:lo + 32, :],
                                     start=True, stop=True).then_inc(gemm_done, 1)
                    g += 1
            e2 = E2.rearrange("p a b c -> p (a b c)")
            pe.wait_ge(gemm_out, g)
            def turn(ft, d):
                u = 2 * ft + d
                if d == 0:
                    pe.wait_ge(vcur_ready, ft + 1)
                    for c in range(TT):
                        mm = nc.tensor.transpose(bank[6][:, c * P:(c + 1) * P], vcur[:, c * P:(c + 1) * P], ident[:, :])
                    mm.then_inc(v_turned, 1)
                pe.wait_ge(ys_out, 3 * u + 1)
                for b in range(NSEQ):
                    for k in range(2):
                        mm = nc.tensor.transpose(bank[7][:, (2 * k + b) * P:(2 * k + b + 1) * P],
                                                 BKt[d][:, k, 2 * b + d, :], ident[:, :])
                mm.then_inc(bk_turned, 1)

            def rhs(ft, d, s):
                u, cs = 2 * ft + d, s if d == 0 else 1 - s
                if s == 0:
                    pe.wait_ge(bktok_ready, u + 1)
                    pe.wait_ge(t_out, 14 * u + 14)
                else:
                    pe.wait_ge(ys_out, 3 * u + 2)
                for b in range(NSEQ):
                    c = 2 * b + cs
                    if s == 1:
                        nc.tensor.matmul(bank[6][:, b * P:(b + 1) * P], ARt[d][:, c, 0, :], Sst[:, b, :],
                                         start=True, stop=False)
                    for h in range(2):
                        i = 2 * b + h
                        mm = nc.tensor.matmul(bank[6][:, i * HD:(i + 1) * HD], Mb[d][:, 2 * c + h, 2, :],
                                              Vtok[:, c, h * HD:h * HD + HD], start=(s == 0), stop=(s == 0 or h == 1))
                mm.then_inc(rhs_done, 1)

            def solve(ft, d, s):
                u, cs = 2 * ft + d, s if d == 0 else 1 - s
                pe.wait_ge(rhs_out, 2 * u + s + 1)
                for i in range(4):
                    c, h = 2 * (i // 2) + cs, i % 2
                    mm = nc.tensor.matmul(bank[6][:, 256 + i * HD:256 + (i + 1) * HD], Tb[d][:, 2 * c + h, 1, :],
                                          RU[:, 0, i * HD:(i + 1) * HD], start=True, stop=True)
                mm.then_inc(u_done, 1)

            def outputs(ft, d, s):
                u, cs = 2 * ft + d, s if d == 0 else 1 - s
                pe.wait_ge(u_out, 2 * u + s + 1)
                if s == 1:
                    pe.wait_ge(ys_out, 3 * u + 3)
                for b in range(NSEQ):
                    c = 2 * b + cs
                    if s == 1:
                        nc.tensor.matmul(bank[7][:, b * P:(b + 1) * P], Sst[:, b, :], ARt[d][:, c, 1, :],
                                         start=True, stop=False)
                    for h in range(2):
                        hs, i = slice(h * HD, h * HD + HD), 2 * b + h
                        U = RU[:, 1, i * HD:(i + 1) * HD]
                        o = bank[7][hs, b * P:(b + 1) * P]
                        nc.tensor.matmul(o, U, Mb[d][:, 2 * c + h, 1, :], start=(s == 0), stop=False)
                        mm = nc.tensor.matmul(o, Vtok[:, c, hs], Mb[d][:, 2 * c + h, 3, :], start=False, stop=True)
                        if s == 0:
                            o = bank[7][hs, 256 + b * HD:256 + (b + 1) * HD]
                            nc.tensor.matmul(o, BKtok[:, 0, b, hs], U, start=True, stop=False)
                            mm = nc.tensor.matmul(o, BKtok[:, 1, b, hs], Vtok[:, c, hs], start=False, stop=True)
                mm.then_inc(ys_done, 1)

            def products_and_inverse(ft, d, last):
                u = 2 * ft + d
                first = isinstance(u, int) and u == 0
                M, Tt = Mb[d], Tb[d]

                def z(l):
                    for q in range(2):
                        if l == 0:
                            pe.wait_ge(m_out, 8 * u + 8)
                        elif l == 1:
                            pe.wait_ge(t_out, 14 * u + q + 1)
                        else:
                            pe.wait_ge(t_copied, 10 * u + 2 * (l - 2) + q + 1)
                        for i in range(4):
                            p = 4 * q + i
                            o = bank[q][:, i * P:(i + 1) * P]
                            if l == 0:
                                mm = nc.tensor.transpose(o, M[:, p, 0, :], ident[:, :])
                            else:
                                mm = nc.tensor.matmul(o, M[:, p, 0, :], Tt[:, p, 0, :], start=True, stop=True)
                        mm.then_inc(z_done, 1)

                def t(l):
                    for q in range(2):
                        pe.wait_ge(z_out, 14 * u + 2 * l + q + 1)
                        for i in range(4):
                            p = 4 * q + i
                            mm = nc.tensor.matmul(bank[2 + q][:, i * P:(i + 1) * P], Zb[:, p, :], Tt[:, p, 1, :],
                                                  start=True, stop=True)
                        mm.then_inc(t_done, 1)
                    if l == LEVELS - 1:
                        return
                    for q in range(2):
                        pe.wait_ge(t_out, 14 * u + 2 * l + q + 1)
                        for i in range(4):
                            mm = nc.tensor.transpose(bank[4 + q][:, i * P:(i + 1) * P], Tt[:, 4 * q + i, 1, :], ident[:, :])
                        mm.then_inc(t_turned, 1)

                pe.wait_ge(prep_ready, u + 2)
                if last is not None:
                    turn(*last)
                for p in range(8):
                    c, hs = p // 2, slice((p % 2) * HD, (p % 2) * HD + HD)
                    if p in (2, 3) and not first:
                        pe.wait_ge(t_out, 14 * u - 1 + (p == 3))
                    if p == 5 and last is not None:
                        rhs(*last, 0)
                    if p >= 6:
                        pe.wait_ge(m_out, 8 * u + p - 5)
                    for k in range(2):
                        mm = nc.tensor.matmul(bank[p % 6][:, k * 256:(k + 1) * 256], BKt[d][hs, k, c, :],
                                              ARt[d][hs, c, :, :].rearrange("p a t -> p (a t)"), start=True, stop=True)
                    mm.then_inc(m_done, 1)
                if last is not None:
                    solve(*last, 0)
                z(0)
                if last is not None:
                    outputs(*last, 0)
                for l in range(1, LEVELS):
                    z(l)
                    if last is not None and l == 1:
                        rhs(*last, 1)
                    if last is not None and l == 2:
                        outputs(*last, 1)
                    t(l)
                    if last is not None and l == 1:
                        solve(*last, 1)
            pe.sem_inc(ys_out, 1)
            pe.wait_ge(sst_zero, 1)
            products_and_inverse(0, 0, None)
            with pe.Fori(0, FT - 1) as ft:
                products_and_inverse(ft, 1, (ft, 0))
                products_and_inverse(ft + 1, 0, (ft, 1))
            products_and_inverse(FT - 1, 1, (FT - 1, 0))
            turn(FT - 1, 1)
            for s in range(2):
                rhs(FT - 1, 1, s)
                solve(FT - 1, 1, s)
                outputs(FT - 1, 1, s)
            pe.wait_ge(y_added, 2 * FT + 1)
            pe.wait_ge(loop_step, FT * LOOP_STEPS)
            for ft in range(FT):
                if ft:
                    pe.wait_ge(gn_out, ft)
                nc.tensor.matmul(bank[0][:, :], blk[:, :], yT[:, ft, :], start=True, stop=True).then_inc(gn_mean, 1)
                nc.tensor.matmul(bank[2][:, :], blk[:, :], kT[:, ft, :], start=True, stop=True)
                nc.tensor.matmul(bank[3][:, :], LUP[64:128, 0, ft * P:(ft + 1) * P], wag[64:128, :],
                                 start=True, stop=True).then_inc(gn_mm, 1)
                pe.wait_ge(gn_sq, ft + 1)
                nc.tensor.matmul(bank[1][:, :], blk[:, :], e2[:, 0:T], start=True, stop=True).then_inc(gn_var, 1)
            pe.wait_ge(gn_out, FT)
            for h in range(2):
                pe.wait_ge(slot_loaded[h], 32)
                W = slot[h].rearrange("p (c f) -> p c f", c=KC)
                for t in range(TT):
                    i = h * TT + t
                    if i >= 4:
                        pe.wait_ge(x_updated, i - 3)
                    for c in range(KC):
                        mm = nc.tensor.matmul(bank[4 + i % 4][:, :], mixT[:, c, t * P:(t + 1) * P], W[:, c, :],
                                              start=(c == 0), stop=(c == KC - 1))
                    mm.then_inc(out_done, 1)
            pe_rest(pe)


_INS = ["x_prompt", "x_sample", "norm_mix", "norm_ffn", "rec_w_in", "rg_conv_w", "rg_conv_b", "rg_wa", "rg_ba",
        "rg_wx", "rg_bx", "rg_lambda", "rw_mu_l", "rw_mu_r", "rw_w0", "rw_w_up", "rw_a0", "rw_a_up", "rw_g_up",
        "rw_k_k", "rw_k_a", "rw_r_k", "rw_ln_w", "rw_ln_b", "rec_w_out", "att_w_in", "att_q_norm", "att_k_norm",
        "att_sink", "att_w_out", "moe_wg1", "moe_bg1", "moe_wg2", "moe_bg2", "moe_w_gate", "moe_w_up", "moe_w_down"]


def kernel(**inputs):
    import concourse.bacc as _bacc
    from concourse.bass_utils import run_bass_kernel_spmd as _run

    nc = _bacc.Bacc("TRN2", target_bir_lowering=False, num_devices=1)
    arrays, args = {}, {}
    for name in _INS:
        v = np.ascontiguousarray(inputs[name])
        arrays[f"in_{name}_dram"] = v
        args[name] = nc.dram_tensor(f"in_{name}_dram", v.shape, mybir.dt.from_np(v.dtype), kind="ExternalInput").ap()
    outs = [nc.dram_tensor(f"out_{i}_dram", (1, SEQ, D), F32, kind="ExternalOutput").ap() for i in range(2)]
    trunk(nc, args, *outs)
    r = _run(nc, [arrays], core_ids=[0])
    return tuple(r.results[0][f"out_{i}_dram"] for i in range(2))
```
